# Optimizing a Trainium2 kernel written in Bass

```python
import jax, jax.numpy as jnp
from jax import lax
import numpy as np

D_MODEL = 1024
BATCH = 1
SEQ = 512
DEPTH = 2

N_MIXERS = 2
N_HEADS = 16
HEAD_DIM = D_MODEL // N_HEADS
Q_BLOCK = 128
SGU_CHUNK = 128
SGU_WIDTH = 2 * D_MODEL
SGU_GROUPS = 16
SGU_GROUP_DIM = SGU_WIDTH // SGU_GROUPS
FFN_HIDDEN = ((8 * D_MODEL // 3 + 255) // 256) * 256
N_ATTN_LAYERS = (DEPTH + 1) // 2
N_SGU_LAYERS = DEPTH // 2
NORM_EPS = 1e-6
LN_EPS = 1e-5

kernel_name = "fox_gmlp_interleaved_hybrid"

def rms_norm(x, w):
    xf = x.astype(jnp.float32)
    y = xf * lax.rsqrt(jnp.mean(xf * xf, axis=-1, keepdims=True) + NORM_EPS)
    return (y * w.astype(jnp.float32)).astype(x.dtype)

def forgetting_attention(h, w_in, b_f, w_out):
    B, S, _ = h.shape
    proj = h @ w_in
    q, k, v, f_logit = jnp.split(proj, [D_MODEL, 2 * D_MODEL, 3 * D_MODEL], axis=-1)
    q = q.reshape(B, S, N_HEADS, HEAD_DIM).transpose(0, 2, 1, 3)
    k = k.reshape(B, S, N_HEADS, HEAD_DIM).transpose(0, 2, 1, 3)
    v = v.reshape(B, S, N_HEADS, HEAD_DIM).transpose(0, 2, 1, 3)
    log_f = jax.nn.log_sigmoid((f_logit + b_f).astype(jnp.float32))
    c = jnp.cumsum(log_f, axis=1).transpose(0, 2, 1)
    n_blk = S // Q_BLOCK
    q_blk = q.reshape(B, N_HEADS, n_blk, Q_BLOCK, HEAD_DIM).transpose(2, 0, 1, 3, 4)
    c_blk = c.reshape(B, N_HEADS, n_blk, Q_BLOCK).transpose(2, 0, 1, 3)
    k_pos = jnp.arange(S)
    scale = HEAD_DIM ** -0.5

    def attend(args):
        qb, cb, start = args
        s = jnp.einsum('bhqd,bhkd->bhqk', qb, k, preferred_element_type=jnp.float32) * scale
        s = s + cb[..., :, None] - c[:, :, None, :]
        q_pos = start + jnp.arange(Q_BLOCK)
        s = jnp.where(k_pos[None, :] <= q_pos[:, None], s, -jnp.inf)
        p = jax.nn.softmax(s, axis=-1).astype(v.dtype)
        return jnp.einsum('bhqk,bhkd->bhqd', p, v)

    o = lax.map(attend, (q_blk, c_blk, jnp.arange(n_blk) * Q_BLOCK))
    o = o.transpose(1, 0, 3, 2, 4).reshape(B, S, D_MODEL)
    return o @ w_out

def spatial_gating_mixer(h, w_in, ln_g, ln_b, w_s, b_s, w_out):
    B, S, _ = h.shape
    z = jax.nn.gelu(h @ w_in, approximate=False)
    u, v = jnp.split(z, 2, axis=-1)
    vf = v.astype(jnp.float32)
    mu = jnp.mean(vf, axis=-1, keepdims=True)
    var = jnp.mean(jnp.square(vf - mu), axis=-1, keepdims=True)
    vn = ((vf - mu) * lax.rsqrt(var + LN_EPS) * ln_g.astype(jnp.float32)
          + ln_b.astype(jnp.float32)).astype(v.dtype)
    vc = vn.reshape(B, S // SGU_CHUNK, SGU_CHUNK, SGU_GROUPS, SGU_GROUP_DIM)
    w_causal = jnp.tril(w_s)
    mixed = jnp.einsum('gts,bcsgd->bctgd', w_causal, vc) + b_s.T[:, :, None]
    gated = u * mixed.reshape(B, S, SGU_WIDTH)
    return gated @ w_out

def swiglu_ffn(h, w_in, w_out):
    g, u = jnp.split(h @ w_in, 2, axis=-1)
    return (jax.nn.silu(g) * u) @ w_out

def setup_inputs(seed: int = 0) -> dict:
    key = jax.random.key(seed)
    ks = jax.random.split(key, 20)
    f32 = jnp.float32
    D = D_MODEL

    def nrm(k, shape, fan_in):
        return jax.random.normal(k, shape, f32) * (fan_in ** -0.5)

    def gain(k, shape):
        return 1.0 + 0.05 * jax.random.normal(k, shape, f32)

    x = jax.random.normal(ks[0], (BATCH, SEQ, D), f32)
    mixer_norm_w = gain(ks[1], (DEPTH, D))
    attn_w_in = nrm(ks[2], (N_ATTN_LAYERS, D, 3 * D + N_HEADS), D)
    attn_b_f = jax.random.uniform(ks[3], (N_ATTN_LAYERS, N_HEADS), f32, 1.0, 6.0)
    attn_w_out = nrm(ks[4], (N_ATTN_LAYERS, D, D), D)
    sgu_w_in = nrm(ks[5], (N_SGU_LAYERS, D, 2 * SGU_WIDTH), D)
    sgu_ln_g = gain(ks[6], (N_SGU_LAYERS, SGU_WIDTH))
    sgu_ln_b = 0.02 * jax.random.normal(ks[7], (N_SGU_LAYERS, SGU_WIDTH), f32)
    sgu_w_s = nrm(ks[8], (N_SGU_LAYERS, SGU_GROUPS, SGU_CHUNK, SGU_CHUNK), SGU_CHUNK)
    sgu_b_s = 1.0 + 0.1 * jax.random.normal(ks[9], (N_SGU_LAYERS, SGU_GROUPS, SGU_CHUNK), f32)
    sgu_w_out = nrm(ks[10], (N_SGU_LAYERS, SGU_WIDTH, D), SGU_WIDTH)
    ffn_norm_w = gain(ks[11], (DEPTH, D))
    ffn_w_in = nrm(ks[12], (DEPTH, D, 2 * FFN_HIDDEN), D)
    ffn_w_out = nrm(ks[13], (DEPTH, FFN_HIDDEN, D), FFN_HIDDEN)
    final_norm_w = gain(ks[14], (D,))
    return {"x": x, "mixer_norm_w": mixer_norm_w, "attn_w_in": attn_w_in,
            "attn_b_f": attn_b_f, "attn_w_out": attn_w_out, "sgu_w_in": sgu_w_in,
            "sgu_ln_g": sgu_ln_g, "sgu_ln_b": sgu_ln_b, "sgu_w_s": sgu_w_s,
            "sgu_b_s": sgu_b_s, "sgu_w_out": sgu_w_out, "ffn_norm_w": ffn_norm_w,
            "ffn_w_in": ffn_w_in, "ffn_w_out": ffn_w_out, "final_norm_w": final_norm_w}

def reference(x, mixer_norm_w, attn_w_in, attn_b_f, attn_w_out, sgu_w_in, sgu_ln_g,
              sgu_ln_b, sgu_w_s, sgu_b_s, sgu_w_out, ffn_norm_w, ffn_w_in, ffn_w_out,
              final_norm_w):
    for i in range(DEPTH):
        h = rms_norm(x, mixer_norm_w[i])
        j = i // N_MIXERS
        if i % N_MIXERS == 0:
            x = x + forgetting_attention(h, attn_w_in[j], attn_b_f[j], attn_w_out[j])
        else:
            x = x + spatial_gating_mixer(h, sgu_w_in[j], sgu_ln_g[j], sgu_ln_b[j],
                                         sgu_w_s[j], sgu_b_s[j], sgu_w_out[j])
        x = x + swiglu_ffn(rms_norm(x, ffn_norm_w[i]), ffn_w_in[i], ffn_w_out[i])
    return rms_norm(x, final_norm_w)


_drawn_inputs = setup_inputs


def setup_inputs(seed=0):
    import zlib

    import numpy as np

    out = dict(_drawn_inputs(seed))
    spreads = {}
    factors = {'sgu_ln_g': 3.29, 'sgu_ln_b': 8.0}
    for name, (base, spread) in spreads.items():
        noise = np.random.default_rng([zlib.crc32(name.encode()), seed]).standard_normal(out[name].shape)
        drawn = base * np.exp(spread * noise) if base else spread * noise
        out[name] = __import__('jax').numpy.asarray(drawn.astype(out[name].dtype))
    for name, factor in factors.items():
        out[name] = (out[name] * factor).astype(out[name].dtype)
    return out
```

```python
from contextlib import ExitStack

import concourse.bass as bass
from concourse import mybir

F32 = mybir.dt.float32
F32R = mybir.dt.float32r
ALU = mybir.AluOpType
ACT = mybir.ActivationFunctionType

P = 128
T = 512
D = 1024
KD = D // P
TT = T // P
H = 16
HD = D // H
PAIRS = H // 2
STEPS = 2 * TT
G = 16
GW = 2 * D
F = 2816
KF = F // P
KG = GW // P
CW = 256
KC = 8
NORM_EPS = 1e-6
LN_EPS = 1e-5
MASKED = 3.0e38

PHASES = [("v", 4, 8), ("qk", 8, 16), ("ao", 4, 8), ("in0", 22, 44), ("out0", 12, 8),
          ("sv", 8, 16), ("su", 8, 16), ("so", 8, 8), ("in1", 22, 44), ("out1", 12, 8)]
CHUNK0, TILE0 = {}, {}
_c = _t = 0
for _name, _chunks, _tiles in PHASES:
    CHUNK0[_name], TILE0[_name] = _c, _t
    _c += _chunks
    _t += _tiles
CHUNKS = _c
RES0 = {"x": 0, "ao": 8, "out0": 16, "so": 24, "out1": 32}
NORM_ROW = {0: 0, 1: 16, 2: 8, 3: 24}


class Count:

    def __init__(self, sem):
        self.sem, self.n, self.turn = sem, 0, 0

    def inc(self, ins):
        ins.then_inc(self.sem, 1)
        self.n += 1
        return self.now()

    def now(self):
        return self.turn + self.n


class Loop:

    def __init__(self, eng, first, end, own=()):
        self.eng, self.first, self.end, self.own = eng, first, end, own

    def __enter__(self):
        self.fori = self.eng.Fori(self.first, self.end)
        self.i = self.fori.__enter__()
        self.start = [c.n for c, _ in self.own]
        for c, rise in self.own:
            c.turn = (self.i - self.first) * rise
        return self.i

    def __exit__(self, *a):
        out = self.fori.__exit__(*a)
        for (c, rise), n in zip(self.own, self.start):
            assert a[0] is not None or c.n - n == rise, (c.sem, c.n - n, rise)
            c.n, c.turn = n + rise * (self.end - self.first), 0
        return out


def ge(eng, sem, value):
    if not isinstance(value, int) or value > 0:
        eng.wait_ge(sem, value)


def wait_tile(eng, e, first_done, pair, w_used, chunk):
    if e == 0:
        eng.wait_ge(first_done, pair + 1)
    else:
        eng.wait_ge(w_used, chunk + 1)


def trunk_kernel(nc, x, mixer_norm_w, attn_w_in, attn_b_f, attn_w_out, sgu_w_in, sgu_ln_g, sgu_ln_b,
                 sgu_w_s, sgu_b_s, sgu_w_out, ffn_norm_w, ffn_w_in, ffn_w_out, final_norm_w, out):
    ctx = ExitStack()
    with ctx:
        top = [32 + nc.sbuf_base]

        def at(name, shape, dt, offset):
            return nc.alloc_sbuf_tensor_at(name, shape, dt, offset=offset)

        def place(name, shape, dt=F32):
            size = 4
            for s in shape[1:]:
                size *= s
            t = at(name, shape, dt, top[0])
            top[0] += -(-size // 32) * 32
            return t

        def sem(name):
            return ctx.enter_context(nc.semaphore(name))

        top[0] = -(-top[0] // 32) * 32
        xT = place("xT", [P, KD, T])
        xh_at = top[0]
        xh = place("xh", [P, KD, T], F32R)
        xl_at = top[0]
        xl = place("xl", [P, KD, T], F32R)
        raw = place("raw", [P, 2, KC, CW])
        wh = place("wh", [P, 2, KC, CW], F32R)
        wl = place("wl", [P, 2, KC, CW], F32R)
        tmp = place("tmp", [P, 4, T])
        rms = place("rms", [P, T])
        sq = place("sq", [P, 2, T])
        sqsum = place("sqsum", [P, T])
        ident = place("ident", [P, P])
        ones = place("ones", [P, P])
        nw = place("nw", [P, 32])
        nw_rows = place("nw_rows", [32, P])
        rcol = place("rcol", [P, TT])
        cols = place("cols", [P, 4, TT])
        eps = place("eps", [P, 4])
        lncol = place("lncol", [P, TT, 2])
        rstd = place("rstd", [P, TT])
        base = top[0]

        V = place("V", [P, TT, D])
        o_at = top[0]
        oh = place("oh", [P, KD, T], F32R)
        ol = place("ol", [P, KD, T], F32R)
        x_tok = at("x_tok", [P, TT, D], F32, o_at)
        qT = place("qT", [P, 2, T])
        kT = place("kT", [P, 2, T])
        c_bc = place("c_bc", [P, 2, 2, T])
        S = place("S", [P, 2, T])
        E = place("E", [P, 2, T])
        ET = place("ET", [P, 2, T])
        o_tok = place("o_tok", [P, TT, P])
        tri = place("tri", [P, T])
        mask = place("mask", [P, P], F32R)
        identr = place("identr", [P, P], F32R)
        mask32 = place("mask32", [P, P])
        wf = place("wf", [P, KD, H])
        wfh = place("wfh", [P, KD, H], F32R)
        wfl = place("wfl", [P, KD, H], F32R)
        bf = place("bf", [P, H])
        fz = place("fz", [P, TT * H])
        fa = place("fa", [P, TT * H])
        cT = place("cT", [H, T])
        smin = place("smin", [P, 2])
        rsum = place("rsum", [P, 2, STEPS])
        rinv = place("rinv", [P, 2, TT])
        ends = [top[0]]

        top[0] = base
        ah = place("ah", [P, KF, T], F32R)
        al = place("al", [P, KF, T], F32R)
        ends.append(top[0])

        top[0] = base
        gh_at = top[0]
        gh = place("gh", [P, KG, T], F32R)
        vt = at("vt", [P, G, TT, P], F32, gh_at)
        gl = place("gl", [P, KG, T], F32R)
        wsT = place("wsT", [P, G, P])
        ws = place("ws", [P, G, P])
        gbc = place("gbc", [P, 2, CW])
        bbc = place("bbc", [P, 2, CW])
        sbc = place("sbc", [P, 2, CW])
        stats = place("stats", [P, TT, 8, 6])
        ends.append(top[0])

        y = at("y", [P, TT, D], F32, xh_at)
        fw = at("fw", [P, D], F32, xl_at)
        assert max(ends) <= nc.sbuf_usable_end, (ends, nc.sbuf_usable_end)

        c_dram = nc.dram_tensor("c_scratch", (H, T), F32).ap()

        bank = [ctx.enter_context(nc.psum_tensor(f"bank{b}", [P, T], F32)) for b in range(8)]
        dense = bank[0:4]
        ps_s = bank[4:6]
        ps_t, ps_o = bank[6], bank[7]

        x_loaded = [sem(f"x_loaded{t}") for t in range(TT)]
        nw_loaded = sem("nw_loaded")
        wf_loaded = sem("wf_loaded")
        ws_loaded = sem("ws_loaded")
        w_loaded = [sem("w_loaded0"), sem("w_loaded1")]
        c_stored = sem("c_stored")
        c_loaded = [sem("c_loaded0"), sem("c_loaded1")]
        ln_loaded = [sem("ln_loaded0"), sem("ln_loaded1")]
        fw_loaded = sem("fw_loaded")
        stored = sem("stored")
        w_hi = sem("w_hi")
        w_lo = sem("w_lo")
        w_used = sem("w_used")
        wf_hi = sem("wf_hi")
        wf_lo = sem("wf_lo")
        first_done = sem("first_done")
        tile_free = sem("tile_free")
        x_turned = sem("x_turned")
        nw_turned = sem("nw_turned")
        nw_ready = sem("nw_ready")
        x_done = sem("x_done")
        xh_done = sem("xh_done")
        xl_done = sem("xl_done")
        sq_done = sem("sq_done")
        sq_added = sem("sq_added")
        summed = sem("summed")
        std_done = sem("std_done")
        r_done = sem("r_done")
        consts = sem("consts")
        identr_done = sem("identr_done")
        f_done = sem("f_done")
        fz_done = sem("fz_done")
        fe_done = sem("fe_done")
        logf_done = sem("logf_done")
        c_summed = sem("c_summed")
        c_ready = sem("c_ready")
        s_done = sem("s_done")
        s_shifted = sem("s_shifted")
        e_done = sem("e_done")
        et_done = sem("et_done")
        et_ready = sem("et_ready")
        pv_done = sem("pv_done")
        o_ready = sem("o_ready")
        o_turned = sem("o_turned")
        oh_done = sem("oh_done")
        ol_done = sem("ol_done")
        silu_done = sem("silu_done")
        gr_done = sem("gr_done")
        ah_done = sem("ah_done")
        al_done = sem("al_done")
        ws_masked = sem("ws_masked")
        ws_turned = sem("ws_turned")
        ws_ready = sem("ws_ready")
        vg_done = sem("vg_done")
        stats_done = sem("stats_done")
        var_ready = sem("var_ready")
        lnstd_done = sem("lnstd_done")
        vc_done = sem("vc_done")
        vn_done = sem("vn_done")
        u_done = sem("u_done")
        mixed = sem("mixed")
        gated = sem("gated")
        gh_done = sem("gh_done")
        gl_done = sem("gl_done")
        y_turned = sem("y_turned")
        y_copied = sem("y_copied")
        mix_read = sem("mix_read")
        y_scaled_dve = sem("y_scaled_dve")
        y_scaled_act = sem("y_scaled_act")
        dve_step = sem("dve_step")
        pool_step = sem("pool_step")
        passed = {e.engine: sem(f"passed{n}") for n, e in enumerate((nc.scalar, nc.vector, nc.gpsimd))}

        w_view = {
            "v": attn_w_in[0].rearrange("(k p) n -> p k n", p=P),
            "qk": attn_w_in[0].rearrange("(k p) n -> p k n", p=P),
            "ao": attn_w_out[0].rearrange("(k p) n -> p k n", p=P),
            "in0": ffn_w_in[0].rearrange("(k p) n -> p k n", p=P),
            "out0": ffn_w_out[0].rearrange("(k p) n -> p k n", p=P),
            "sv": sgu_w_in[0].rearrange("(k p) n -> p k n", p=P),
            "su": sgu_w_in[0].rearrange("(k p) n -> p k n", p=P),
            "so": sgu_w_out[0].rearrange("(k p) n -> p k n", p=P),
            "in1": ffn_w_in[1].rearrange("(k p) n -> p k n", p=P),
            "out1": ffn_w_out[1].rearrange("(k p) n -> p k n", p=P),
        }

        def apart(eng):
            eng.sem_inc(passed[eng.engine], 1)

        block = ctx.enter_context(nc.Block())

        @block.sync
        def _(sp):
            for t in range(TT):
                sp.dma_start(x_tok[:, t, :], x[0, t * P:(t + 1) * P, :]).then_inc(x_loaded[t], 16)
            sp.dma_start(nw_rows[0:16, :], mixer_norm_w.rearrange("i (k p) -> (i k) p", p=P)).then_inc(nw_loaded, 16)
            sp.dma_start(nw_rows[16:32, :], ffn_norm_w.rearrange("i (k p) -> (i k) p", p=P)).then_inc(nw_loaded, 16)

            def load(slot, n, parts):
                ge(sp, w_lo, n - 1)
                for dst, src in parts:
                    sp.dma_start(dst, src).then_inc(w_loaded[slot], 16)

            def whole(phase, slot, n, col, k0=0, ks=KC):
                h = ks // 2
                load(slot, n, [(raw[:, slot, 0:h, :], w_view[phase][:, k0:k0 + h, bass.ds(col, CW)]),
                               (raw[:, slot, h:ks, :], w_view[phase][:, k0 + h:k0 + ks, bass.ds(col, CW)])])

            for c in range(4):
                whole("v", c % 2, c, 2 * D + c * CW)
                if c == 1:
                    sp.dma_start(wf[:, :, :], w_view["v"][:, :, 3 * D:3 * D + H]).then_inc(wf_loaded, 16)
                    sp.dma_start(bf[:, :], attn_b_f[0:1, :].partition_broadcast(P)).then_inc(wf_loaded, 16)

            def load_qk(p, slot):
                w = w_view["qk"]
                load(slot, CHUNK0["qk"] + p, [(raw[:, slot, :, 0:P], w[:, :, bass.ds(p * P, P)]),
                                              (raw[:, slot, :, P:CW], w[:, :, bass.ds(p * P + D, P)])])

            def load_c(p, slot):
                ge(sp, s_shifted, STEPS * (p - 1))
                sp.dma_start(c_bc[:, slot, :, :], c_dram[bass.ds(p * 2, 2), :].partition_broadcast(P))\
                    .then_inc(c_loaded[slot], 16)

            load_qk(0, 0)
            load_qk(1, 1)
            sp.wait_ge(c_ready, 1)
            sp.dma_start(c_dram, cT[:, :]).then_inc(c_stored, 16)
            sp.wait_ge(c_stored, 16)
            load_c(0, 0)
            load_c(1, 1)
            with Loop(sp, 0, PAIRS // 2 - 1) as i:
                for b in range(2):
                    load_qk(i * 2 + (b + 2), b)
                    load_c(i * 2 + (b + 2), b)

            def stream(phase, turns, body):
                with Loop(sp, 0, turns) as i:
                    body(i, CHUNK0[phase])

            def columns(phase, col0=0):
                def body(i, n0):
                    for b in range(2):
                        whole(phase, b, i * 2 + (n0 + b), i * (2 * CW) + (col0 + b * CW))
                return body

            def ffn_in(phase):
                def body(i, n0):
                    for b in range(2):
                        whole(phase, b, i * 2 + (n0 + b), i * CW + b * F)
                return body

            def deep(phase, cuts):
                def body(i, n0):
                    n = 0
                    for b in range(2):
                        k0 = 0
                        for ks in cuts:
                            whole(phase, n % 2, i * (2 * len(cuts)) + (n0 + n), i * (2 * CW) + b * CW, k0, ks)
                            k0 += ks
                            n += 1
                return body

            stream("ao", 2, columns("ao"))
            stream("in0", KF // 2, ffn_in("in0"))
            stream("out0", 2, deep("out0", (8, 8, 6)))
            sp.wait_ge(w_used, CHUNK0["sv"])
            sp.dma_start(ws[:, :, :], sgu_w_s[0].rearrange("g t s -> t g s")).then_inc(ws_loaded, 16)
            stream("sv", 4, columns("sv", GW))

            def load_ln(c, slot):
                ge(sp, gated, 2 * (c - 1))
                for dst, src in ((gbc, sgu_ln_g[0:1, bass.ds(c * CW, CW)]), (bbc, sgu_ln_b[0:1, bass.ds(c * CW, CW)]),
                                 (sbc, sgu_b_s.rearrange("l g t -> l (g t)")[:, bass.ds(c * CW, CW)])):
                    sp.dma_start(dst[:, slot, :], src.partition_broadcast(P)).then_inc(ln_loaded[slot], 16)

            for b in range(2):
                load_ln(b, b)
                whole("su", b, CHUNK0["su"] + b, b * CW)
            with Loop(sp, 1, 4) as i:
                for b in range(2):
                    whole("su", b, i * 2 + (CHUNK0["su"] + b), i * (2 * CW) + b * CW)
                    load_ln(i * 2 + b, b)
            stream("so", 2, deep("so", (8, 8)))
            stream("in1", KF // 2, ffn_in("in1"))
            stream("out1", 2, deep("out1", (8, 8, 6)))

            for t in range(TT):
                sp.wait_ge((y_scaled_dve, y_scaled_act)[t % 2], t // 2 + 1)
                sp.dma_start(out[0, t * P:(t + 1) * P, :], y[:, t, :]).then_inc(stored, 16)
            sp.wait_ge(stored, 16 * TT)

        @block.gpsimd
        def _(pool):
            step = Count(pool_step)
            nc.gpsimd.memset(ones[:, :], 1.0).then_inc(consts, 1)
            for e, value in enumerate((NORM_EPS, LN_EPS, 1.0)):
                nc.gpsimd.memset(eps[:, e:e + 1], value).then_inc(consts, 1)
            step.inc(nc.gpsimd.memset(ident[:, :], 0.0))
            step.inc(nc.gpsimd.memset(tri[:, :], 1.0))
            step.inc(nc.gpsimd.memset(mask32[:, :], 0.0))
            pool.wait_ge(pool_step, step.now())
            nc.gpsimd.affine_select(out=ident[:, :], in_=ident[:, :], compare_op=ALU.not_equal, fill=1.0, base=0,
                                    pattern=[[-1, P]], channel_multiplier=1).then_inc(consts, 1)
            nc.gpsimd.affine_select(out=tri[:, :], in_=tri[:, :], compare_op=ALU.is_ge, fill=0.0, base=0,
                                    pattern=[[1, T]], channel_multiplier=-1).then_inc(consts, 1)
            nc.gpsimd.affine_select(out=mask32[:, :], in_=mask32[:, :], compare_op=ALU.is_ge, fill=MASKED, base=0,
                                    pattern=[[-1, P]], channel_multiplier=1).then_inc(consts, 1)

            def clear_sum(norm):
                ge(pool, summed, norm)
                step.inc(nc.gpsimd.memset(sqsum[:, :], 0.0))
                pool.wait_ge(pool_step, step.now())

            def add_square(r, slot):
                pool.wait_ge(sq_done, r + 1)
                ge(pool, sq_added, r)
                nc.gpsimd.tensor_tensor(sqsum[:, :], sqsum[:, :], sq[:, slot, :], ALU.add).then_inc(sq_added, 1)

            def sum_pass(name, norm):
                clear_sum(norm)
                with Loop(pool, 0, KD // 2) as i:
                    for b in range(2):
                        add_square(i * 2 + (RES0[name] + b), b)

            def ffn(layer):
                with Loop(pool, 0, KF // 2) as i:
                    for b in range(2):
                        pool.wait_ge(silu_done, i * 2 + (layer * KF + b + 1))
                        nc.gpsimd.tensor_tensor(tmp[:, b, :], tmp[:, b, :], rms[:, :], ALU.mult).then_inc(gr_done, 1)

            clear_sum(0)
            for k in range(KD):
                add_square(k, k % 2)
            sum_pass("ao", 1)
            ffn(0)
            sum_pass("out0", 2)
            pool.wait_ge(ws_loaded, 16)
            nc.gpsimd.affine_select(out=ws[:, :, :], in_=ws[:, :, :], compare_op=ALU.is_ge, fill=0.0, base=0,
                                    pattern=[[0, G], [-1, P]], channel_multiplier=1).then_inc(ws_masked, 1)

            def gains(c, slot):
                pool.wait_ge(vc_done, (c + 1) * TT)
                pool.wait_ge(ln_loaded[slot], c * 24 + (48 - 24 * slot))
                for g in range(2):
                    v = vt[:, bass.ds(c * 2 + g, 1), :, :].rearrange("p a t d -> p (a t) d")
                    gain = gbc[:, slot, g * P:(g + 1) * P].unsqueeze(1).broadcast_to([P, TT, P])
                    bias = bbc[:, slot, g * P:(g + 1) * P].unsqueeze(1).broadcast_to([P, TT, P])
                    step.inc(nc.gpsimd.tensor_tensor(v, v, gain, ALU.mult))
                    pool.wait_ge(pool_step, step.now())
                    apart(pool)
                    nc.gpsimd.tensor_tensor(v, v, bias, ALU.add).then_inc(vn_done, 1)

            with Loop(pool, 0, 4, own=[(step, 4)]) as i:
                for b in range(2):
                    gains(i * 2 + b, b)
            sum_pass("so", 3)
            ffn(1)
            sum_pass("out1", 4)

        @block.scalar
        def _(act):
            def upper(slot, n, ks=KC, parts=1):
                for _ in upper_parts(slot, n, ks, parts):
                    pass

            def upper_parts(slot, n, ks=KC, parts=1):
                act.wait_ge(w_loaded[slot], n * 16 + (32 - 16 * slot))
                ge(act, w_used, n - 1)
                for q in range(parts):
                    k0, k1 = ks * q // parts, ks * (q + 1) // parts
                    ins = nc.scalar.activation(wh[:, slot, k0:k1, :], raw[:, slot, k0:k1, :], ACT.Copy)
                    if q == parts - 1:
                        ins.then_inc(w_hi, 1)
                    yield

            def residual(name, k, slot, norm):
                r = k + RES0[name]
                if name == "x":
                    act.wait_ge(x_done, k + 1)
                else:
                    act.wait_ge(tile_free, k + (TILE0[name] + 1))
                if norm < 4:
                    w = nw[:, bass.ds(k + NORM_ROW[norm], 1)]
                    nc.scalar.activation(xh[:, bass.ds(k, 1), :].rearrange("p a t -> p (a t)"),
                                         xT[:, bass.ds(k, 1), :].rearrange("p a t -> p (a t)"),
                                         ACT.Copy, scale=w).then_inc(xh_done, 1)
                ge(act, sq_added, r - 1)
                apart(act)
                nc.scalar.activation(sq[:, slot, :], xT[:, bass.ds(k, 1), :].rearrange("p a t -> p (a t)"),
                                     ACT.Square).then_inc(sq_done, 1)

            def norm_roots(norm, rows, columns):
                act.wait_ge(summed, norm + 1)
                if rows:
                    nc.scalar.activation(tmp[:, 0, :], ps_s[0][:, :], ACT.Sqrt, bias=eps[:, 0:1], scale=1.0 / D)\
                        .then_inc(std_done, 1)
                if columns:
                    nc.scalar.activation(cols[:, 0, :], ps_s[1][:, 0:TT], ACT.Sqrt, bias=eps[:, 0:1], scale=1.0 / D)\
                        .then_inc(std_done, 1)

            act.wait_ge(consts, 7)
            act.wait_ge(nw_ready, 1)
            for k in range(KD):
                residual("x", k, k % 2, 0)
                if k == 3:
                    upper(0, 0)
            upper(1, 1)
            act.wait_ge(wf_loaded, 32)
            nc.scalar.activation(wfh[:, :, :], wf[:, :, :], ACT.Copy).then_inc(wf_hi, 1)
            norm_roots(0, True, True)
            nc.scalar.activation(mask[:, :], mask32[:, :], ACT.Copy).then_inc(identr_done, 1)
            nc.scalar.activation(identr[:, :], ident[:, :], ACT.Copy).then_inc(identr_done, 1)
            act.wait_ge(fz_done, 1)
            nc.scalar.activation(fa[:, :], fa[:, :], ACT.Exp, scale=-1.0).then_inc(fe_done, 1)
            act.wait_ge(fe_done, 1)
            nc.scalar.activation(fa[:, :], fa[:, :], ACT.Ln, bias=eps[:, 2:3]).then_inc(fe_done, 1)
            for c in range(4):
                upper(c % 2, c + 2)

            def exps(p, s, b):
                i, n = s % TT, (s % TT + 1) * P
                S0 = p * STEPS + s
                act.wait_ge(s_shifted, S0 + 1)
                ge(act, et_done, S0 - 1)
                nc.scalar.activation(E[:, s % 2, 0:n], S[:, s % 2, 0:n], ACT.Exp, bias=smin[:, s % 2:s % 2 + 1],
                                     scale=-1.0, accum_out=rsum[:, b, s:s + 1]).then_inc(e_done, 1)

            def copy_turned(p, s):
                n = (s % TT + 1) * P
                S0 = p * STEPS + s
                act.wait_ge(et_done, S0 + 1)
                ge(act, pv_done, S0 - 1)
                nc.scalar.activation(ET[:, s % 2, 0:n], ps_t[:, 0:n], ACT.Copy).then_inc(et_ready, 1)

            def out_upper(p):
                act.wait_ge(o_turned, p + 1)
                nc.scalar.activation(oh[:, bass.ds(p, 1), :].rearrange("p a t -> p (a t)"), ps_t[:, :], ACT.Copy)\
                    .then_inc(oh_done, 1)

            def attend(p, b, first, last):
                split = upper_parts(b, p + (CHUNK0["qk"] + 2), KC, TT)
                for s in range(STEPS):
                    exps(p, s, b)
                    if s == 5 and not first:
                        out_upper(p - 1)
                    if s >= 1:
                        copy_turned(p, s - 1)
                    elif not first:
                        copy_turned(p - 1, STEPS - 1)
                    next(split, None)
                if last:
                    copy_turned(p, STEPS - 1)
                    out_upper(p)

            attend(0, 0, True, False)
            with Loop(act, 0, PAIRS // 2 - 1) as i:
                attend(i * 2 + 1, 1, False, False)
                attend(i * 2 + 2, 0, False, False)
            attend(PAIRS - 1, 1, False, True)

            def residual_pass(name, norm, cuts):
                per = 2 * len(cuts)
                with Loop(act, 0, 2) as i:
                    for n in range(per):
                        if n % len(cuts) == len(cuts) - 1:
                            for e in range(2):
                                k = i * 4 + (n // len(cuts) * 2 + e)
                                residual(name, k, e, norm)
                        size = cuts[(n + 2) % len(cuts)] if n + 2 < per else KC
                        upper(n % 2, i * per + (CHUNK0[name] + n + 2), size)

            def ffn_in(name, layer, norm):
                norm_roots(norm, True, False)
                with Loop(act, 0, KF // 2) as j:
                    for e in range(2):
                        act.wait_ge(tile_free, j * 4 + (TILE0[name] + e + 1))
                        nc.scalar.activation(tmp[:, e, :], tmp[:, e, :], ACT.Silu).then_inc(silu_done, 1)
                    upper(0, j * 2 + (CHUNK0[name] + 2))
                    for e in range(2):
                        act.wait_ge(tile_free, j * 4 + (TILE0[name] + e + 3))
                        nc.scalar.activation(ah[:, bass.ds(j * 2 + e, 1), :].rearrange("p a t -> p (a t)"),
                                             tmp[:, 2 + e, :], ACT.Copy).then_inc(ah_done, 1)
                    upper(1, j * 2 + (CHUNK0[name] + 3))

            residual_pass("ao", 1, (8,))
            ffn_in("in0", 0, 1)
            residual_pass("out0", 2, (8, 8, 6))

            norm_roots(2, True, True)
            with Loop(act, 0, 4) as i:
                for b in range(2):
                    for t in range(TT):
                        act.wait_ge(tile_free, i * 4 + (TILE0["sv"] + 2 * b + t // 2 + 1))
                        v = vt[:, bass.ds(i * 4 + 2 * b, 2), t, :]
                        nc.scalar.activation(v, v, ACT.Gelu).then_inc(vg_done, 1)
                    upper(b, i * 2 + (CHUNK0["sv"] + b + 2))
            act.wait_ge(var_ready, 1)
            nc.scalar.activation(cols[:, 0, :], lncol[:, :, 1], ACT.Sqrt, bias=eps[:, 1:2]).then_inc(lnstd_done, 1)

            with Loop(act, 0, 4) as i:
                for b in range(2):
                    for e in range(2):
                        act.wait_ge(tile_free, i * 4 + (TILE0["su"] + 2 * b + e + 1))
                        nc.scalar.activation(tmp[:, e, :], tmp[:, e, :], ACT.Gelu).then_inc(u_done, 1)
                    for e in range(2):
                        act.wait_ge(gated, i * 4 + (2 * b + e + 1))
                        nc.scalar.activation(gh[:, bass.ds(i * 4 + (2 * b + e), 1), :].rearrange("p a t -> p (a t)"),
                                             tmp[:, 2 + e, :], ACT.Copy).then_inc(gh_done, 1)
                    upper(b, i * 2 + (CHUNK0["su"] + b + 2))
            residual_pass("so", 3, (8, 8))
            ffn_in("in1", 1, 3)

            for n in range(12):
                if n % 3 == 2:
                    for e in range(2):
                        k = n // 3 * 2 + e
                        residual("out1", k, e, 4)
                if n + 2 < 12:
                    upper(n % 2, CHUNK0["out1"] + n + 2, 6 if n % 3 == 0 else KC)
                if n == 0:
                    act.wait_ge(w_used, CHUNK0["out1"])
                    act.dma_start(fw[:, :], final_norm_w.rearrange("(a d) -> a d", a=1).partition_broadcast(P))\
                        .then_inc(fw_loaded, 16)
            norm_roots(4, False, True)
            act.wait_ge(r_done, 5)
            act.wait_ge(y_copied, KD)
            for t in (1, 3):
                nc.scalar.activation(y[:, t, :], y[:, t, :], ACT.Copy, scale=rcol[:, t:t + 1]).then_inc(y_scaled_act, 1)

        @block.vector
        def _(dve):
            step = Count(dve_step)

            def chained(ins):
                dve.wait_ge(dve_step, step.inc(ins))

            def tile_of(buf, k):
                return buf[:, bass.ds(k, 1), :].rearrange("p a t -> p (a t)")

            def lower_parts(slot, n, ks=KC, parts=1):
                dve.wait_ge(w_hi, n + 1)
                ge(dve, w_used, n - 1)
                for q in range(parts):
                    k0, k1 = ks * q // parts, ks * (q + 1) // parts
                    ins = nc.vector.tensor_tensor(wl[:, slot, k0:k1, :], raw[:, slot, k0:k1, :],
                                                  wh[:, slot, k0:k1, :].bitcast(F32), ALU.subtract)
                    if q == parts - 1:
                        ins.then_inc(w_lo, 1)
                    yield

            def lower(slot, n, ks=KC):
                for _ in lower_parts(slot, n, ks):
                    pass

            def input_lower(r, k, norm):
                dve.wait_ge(xh_done, r + 1)
                nc.vector.scalar_tensor_tensor(out=tile_of(xl, k), in0=tile_of(xT, k),
                                               scalar=nw[:, bass.ds(k + NORM_ROW[norm], 1)],
                                               in1=tile_of(xh, k).bitcast(F32), op0=ALU.mult,
                                               op1=ALU.subtract).then_inc(xl_done, 1)

            def newton(out_, mean, root, r, t):
                chained(nc.vector.reciprocal(r, root))
                chained(nc.vector.tensor_tensor(t, r, r, ALU.mult))
                chained(nc.vector.tensor_tensor(t, t, mean, ALU.mult))
                chained(nc.vector.tensor_scalar(t, t, -0.5, 1.5, ALU.mult, ALU.add))
                return nc.vector.tensor_tensor(out_, r, t, ALU.mult)

            roots = [0]

            def norm_scale(norm, rows, columns):
                dve.wait_ge(summed, norm + 1)
                if rows:
                    roots[0] += 1
                    dve.wait_ge(std_done, roots[0])
                    chained(nc.vector.tensor_scalar(tmp[:, 1, :], ps_s[0][:, :], 1.0 / D, NORM_EPS, ALU.mult, ALU.add))
                    ins = newton(rms[:, :], tmp[:, 1, :], tmp[:, 0, :], tmp[:, 2, :], tmp[:, 3, :])
                if columns:
                    if rows:
                        chained(ins)
                    roots[0] += 1
                    dve.wait_ge(std_done, roots[0])
                    chained(nc.vector.tensor_scalar(cols[:, 1, :], ps_s[1][:, 0:TT], 1.0 / D, NORM_EPS,
                                                    ALU.mult, ALU.add))
                    ins = newton(rcol[:, :], cols[:, 1, :], cols[:, 0, :], cols[:, 2, :], cols[:, 3, :])
                ins.then_inc(r_done, 1)
                dve.wait_ge(r_done, norm + 1)

            dve.wait_ge(consts, 7)
            dve.wait_ge(nw_turned, 1)
            nc.vector.tensor_copy(nw[:, :], ps_o[:, 0:32]).then_inc(nw_ready, 1)
            dve.wait_ge(nw_ready, 1)
            for k in range(KD):
                dve.wait_ge(x_turned, k + 1)
                nc.vector.tensor_copy(xT[:, k, :], bank[4 + k % 4][:, :]).then_inc(x_done, 1)
                input_lower(k, k, 0)
                if k == 4:
                    lower(0, 0)
            lower(1, 1)
            dve.wait_ge(wf_hi, 1)
            nc.vector.tensor_tensor(wfl[:, :, :], wf[:, :, :], wfh[:, :, :].bitcast(F32), ALU.subtract)\
                .then_inc(wf_lo, 1)
            norm_scale(0, True, True)

            def values(c, m):
                for t in range(TT):
                    if t % 2 == 0:
                        wait_tile(dve, t // 2, first_done, m // 2, w_used, c)
                    ins = nc.vector.tensor_scalar(V[:, t, c * CW:(c + 1) * CW],
                                                  dense[(m + t // 2) % 4][:, t % 2 * CW:(t % 2 + 1) * CW],
                                                  rcol[:, t:t + 1], None, ALU.mult)
                    if t % 2 == 1:
                        ins.then_inc(tile_free, 1)

            for c in range(4):
                values(c, TILE0["v"] + 2 * c)
                if c == 0:
                    dve.wait_ge(f_done, 1)
                    for t in range(TT):
                        step.inc(nc.vector.scalar_tensor_tensor(
                            out=fz[:, t * H:(t + 1) * H], in0=ps_o[:, t * H:(t + 1) * H], scalar=rcol[:, t:t + 1],
                            in1=bf[:, :], op0=ALU.mult, op1=ALU.add))
                    dve.wait_ge(dve_step, step.now())
                    nc.vector.scalar_tensor_tensor(out=fa[:, :], in0=fz[:, :], scalar=-1.0, in1=fz[:, :],
                                                   op0=ALU.mult, op1=ALU.max).then_inc(fz_done, 1)
                if c == 1:
                    dve.wait_ge(fe_done, 2)
                    nc.vector.scalar_tensor_tensor(out=fz[:, :], in0=fz[:, :], scalar=0.0, in1=fa[:, :],
                                                   op0=ALU.min, op1=ALU.subtract).then_inc(logf_done, 1)
                if c == 3:
                    dve.wait_ge(c_summed, 1)
                    nc.vector.tensor_copy(cT[:, :], ps_t[0:H, :]).then_inc(c_ready, 1)
                lower(c % 2, c + 2)

            def queries(p, b):
                dve.wait_ge(first_done, p + (TILE0["qk"] // 2 + 1))
                nc.vector.scalar_tensor_tensor(out=qT[:, b, :], in0=dense[2 * b][:, :], scalar=-(HD ** -0.5),
                                               in1=rms[:, :], op0=ALU.mult, op1=ALU.mult)\
                    .then_inc(tile_free, 1)

            def keys(p, b):
                dve.wait_ge(w_used, p + (CHUNK0["qk"] + 1))
                nc.vector.tensor_tensor(kT[:, b, :], dense[2 * b + 1][:, :], rms[:, :], ALU.mult)\
                    .then_inc(tile_free, 1)

            def shift(p, s, b):
                i, n = s % TT, (s % TT + 1) * P
                S0 = p * STEPS + s
                dve.wait_ge(s_done, S0 + 1)
                if s == 0:
                    dve.wait_ge(c_loaded[b], p * 8 + (16 - 8 * b))
                ge(dve, e_done, S0 - 1)
                apart(dve)
                nc.vector.tensor_tensor_reduce(S[:, s % 2, 0:n], ps_s[s % 2][:, 0:n], c_bc[:, b, s // TT, 0:n],
                                               1.0, 3.4e38, ALU.add, ALU.min, smin[:, s % 2:s % 2 + 1])\
                    .then_inc(s_shifted, 1)

            def normalised(p, a, b):
                dve.wait_ge(e_done, p * STEPS + (a + 1) * TT)
                chained(nc.vector.reciprocal(rinv[:, b, :], rsum[:, b, a * TT:(a + 1) * TT]))
                dve.wait_ge(pv_done, p * STEPS + (a + 1) * TT)
                nc.vector.tensor_tensor(o_tok[:, :, a * HD:(a + 1) * HD],
                                        ps_o[:, a * TT * HD:(a + 1) * TT * HD].rearrange("p (i d) -> p i d", d=HD),
                                        rinv[:, b, :].unsqueeze(2).broadcast_to([P, TT, HD]), ALU.mult)\
                    .then_inc(o_ready, 1)

            def out_lower(p):
                dve.wait_ge(oh_done, p + 1)
                nc.vector.tensor_tensor(tile_of(ol, p), ps_t[:, :], tile_of(oh, p).bitcast(F32), ALU.subtract)\
                    .then_inc(ol_done, 1)

            def attend(p, b, first, last):
                split = lower_parts(b, p + (CHUNK0["qk"] + 2), KC, TT)
                for s in range(STEPS):
                    shift(p, s, b)
                    if s == 2 and not first:
                        normalised(p - 1, 1, 1 - b)
                    if s == 5:
                        if not first:
                            out_lower(p - 1)
                        if not last:
                            queries(p + 1, 1 - b)
                    if s == 6:
                        normalised(p, 0, b)
                    if s >= TT:
                        next(split)
                if not last:
                    keys(p + 1, 1 - b)
                else:
                    normalised(p, 1, b)
                    out_lower(p)

            queries(0, 0)
            keys(0, 0)
            attend(0, 0, True, False)
            with Loop(dve, 0, PAIRS // 2 - 1, own=[(step, 4)]) as i:
                attend(i * 2 + 1, 1, False, False)
                attend(i * 2 + 2, 0, False, False)
            attend(PAIRS - 1, 1, False, True)

            def residual(name, k, e, bank_, pair, chunk, norm):
                wait_tile(dve, e, first_done, pair + TILE0[name] // 2, w_used, chunk + CHUNK0[name])
                nc.vector.tensor_tensor(tile_of(xT, k), tile_of(xT, k), dense[bank_][:, :], ALU.add)\
                    .then_inc(tile_free, 1)
                if norm < 4:
                    input_lower(k + RES0[name], k, norm)

            def residual_pass(name, norm, cuts):
                per = 2 * len(cuts)
                with Loop(dve, 0, 2) as i:
                    for n in range(per):
                        if n % len(cuts) == len(cuts) - 1:
                            for e in range(2):
                                t = n // len(cuts) * 2 + e
                                residual(name, i * 4 + t, e, t, i * 2 + t // 2, i * per + n, norm)
                        size = cuts[(n + 2) % len(cuts)] if n + 2 < per else KC
                        lower(n % 2, i * per + (CHUNK0[name] + n + 2), size)

            def ffn_in(name, layer, norm):
                norm_scale(norm, True, False)
                with Loop(dve, 0, KF // 2) as j:
                    for e in range(2):
                        wait_tile(dve, e, first_done, j * 2 + TILE0[name] // 2, w_used, j * 2 + CHUNK0[name])
                        nc.vector.tensor_tensor(tmp[:, e, :], dense[e][:, :], rms[:, :], ALU.mult)\
                            .then_inc(tile_free, 1)
                    lower(0, j * 2 + (CHUNK0[name] + 2))
                    for e in range(2):
                        wait_tile(dve, e, first_done, j * 2 + (TILE0[name] // 2 + 1), w_used,
                                  j * 2 + (CHUNK0[name] + 1))
                        dve.wait_ge(gr_done, j * 2 + (layer * KF + e + 1))
                        nc.vector.tensor_tensor(tmp[:, 2 + e, :], dense[2 + e][:, :], tmp[:, e, :], ALU.mult)\
                            .then_inc(tile_free, 1)
                    for e in range(2):
                        dve.wait_ge(ah_done, j * 2 + (layer * KF + e + 1))
                        nc.vector.tensor_tensor(tile_of(al, j * 2 + e), tmp[:, 2 + e, :],
                                                tile_of(ah, j * 2 + e).bitcast(F32), ALU.subtract)\
                            .then_inc(al_done, 1)
                    lower(1, j * 2 + (CHUNK0[name] + 3))

            residual_pass("ao", 1, (8,))
            ffn_in("in0", 0, 1)
            residual_pass("out0", 2, (8, 8, 6))

            norm_scale(2, True, True)
            with Loop(dve, 0, 4) as i:
                for b in range(2):
                    for t in range(TT):
                        if t % 2 == 0:
                            wait_tile(dve, t // 2, first_done, i * 2 + (TILE0["sv"] // 2 + b), w_used,
                                      i * 2 + (CHUNK0["sv"] + b))
                        ins = nc.vector.tensor_scalar(
                            vt[:, bass.ds(i * 4 + 2 * b, 2), t, :],
                            dense[2 * b + t // 2][:, t % 2 * CW:(t % 2 + 1) * CW].rearrange("p (g d) -> p g d", d=P),
                            rcol[:, t:t + 1], None, ALU.mult)
                        if t % 2 == 1:
                            ins.then_inc(tile_free, 1)
                    for t in range(TT):
                        dve.wait_ge(vg_done, i * (2 * TT) + (b * TT + t + 1))
                        ins = nc.vector.bn_stats(stats[:, t, bass.ds(i * 2 + b, 1), :].rearrange("p a s -> p (a s)"),
                                                 vt[:, bass.ds(i * 4 + 2 * b, 2), t, :])
                    ins.then_inc(stats_done, 1)
                    lower(b, i * 2 + (CHUNK0["sv"] + b + 2))
            for q in range(4):
                dve.wait_ge(ws_turned, q + 1)
                nc.vector.tensor_copy(wsT[:, 4 * q:4 * q + 4, :],
                                      bank[6 + q % 2].rearrange("p (g t) -> p g t", t=P)).then_inc(ws_ready, 1)
            dve.wait_ge(stats_done, 8)
            for t in range(TT):
                ins = nc.vector.bn_aggr(lncol[:, t, :], stats[:, t, :, :].rearrange("p c s -> p (c s)"))
            ins.then_inc(var_ready, 1)
            dve.wait_ge(var_ready, 1)
            chained(nc.vector.tensor_scalar(cols[:, 1, :], lncol[:, :, 1], LN_EPS, None, ALU.add))
            dve.wait_ge(lnstd_done, 1)
            chained(newton(rstd[:, :], cols[:, 1, :], cols[:, 0, :], cols[:, 2, :], cols[:, 3, :]))

            def centred(c):
                for t in range(TT):
                    v = vt[:, bass.ds(c * 2, 2), t, :]
                    nc.vector.tensor_scalar(v, v, lncol[:, t, 0:1], rstd[:, t:t + 1], ALU.subtract, ALU.mult)\
                        .then_inc(vc_done, 1)

            def gate(c, b, ahead):
                for e in range(2):
                    wait_tile(dve, e, first_done, c + TILE0["su"] // 2, w_used, c + CHUNK0["su"])
                    nc.vector.tensor_tensor(tmp[:, e, :], dense[2 * b + e][:, :], rms[:, :], ALU.mult)\
                        .then_inc(tile_free, 1)
                if ahead:
                    centred(c + 1)
                dve.wait_ge(ln_loaded[b], c * 24 + (48 - 24 * b))
                ge(dve, gl_done, c * 2)
                for e in range(2):
                    dve.wait_ge(mixed, c * 2 + (e + 1))
                    t = tmp[:, 2 + e, :].rearrange("p (c t) -> p c t", t=P)
                    nc.vector.tensor_tensor(t, ps_s[e].rearrange("p (c t) -> p c t", t=P),
                                            sbc[:, b, e * P:(e + 1) * P].unsqueeze(1).broadcast_to([P, TT, P]),
                                            ALU.add).then_inc(mix_read, 1)
                for e in range(2):
                    dve.wait_ge(mix_read, c * 2 + (e + 1))
                    dve.wait_ge(u_done, c * 2 + (e + 1))
                    nc.vector.tensor_tensor(tmp[:, 2 + e, :], tmp[:, 2 + e, :], tmp[:, e, :], ALU.mult)\
                        .then_inc(gated, 1)
                for e in range(2):
                    dve.wait_ge(gh_done, c * 2 + (e + 1))
                    nc.vector.tensor_tensor(tile_of(gl, c * 2 + e), tmp[:, 2 + e, :],
                                            tile_of(gh, c * 2 + e).bitcast(F32), ALU.subtract).then_inc(gl_done, 1)
                lower(b, c + (CHUNK0["su"] + 2))

            centred(0)
            gate(0, 0, True)
            gate(1, 1, True)
            with Loop(dve, 1, 3) as i:
                gate(i * 2, 0, True)
                gate(i * 2 + 1, 1, True)
            gate(6, 0, True)
            gate(7, 1, False)
            residual_pass("so", 3, (8, 8))
            ffn_in("in1", 1, 3)

            def result(k):
                dve.wait_ge(y_turned, k + 1)
                nc.vector.tensor_tensor(y[:, :, k * P:(k + 1) * P], bank[4 + k % 4].rearrange("p (t d) -> p t d", d=P),
                                        fw[:, k * P:(k + 1) * P].unsqueeze(1).broadcast_to([P, TT, P]), ALU.mult)\
                    .then_inc(y_copied, 1)

            for n in range(12):
                if n % 3 == 2:
                    if n == 5:
                        dve.wait_ge(fw_loaded, 16)
                    if n > 2:
                        for e in range(2):
                            result(n // 3 * 2 - 2 + e)
                    for e in range(2):
                        k = n // 3 * 2 + e
                        residual("out1", k, e, k % 4, k // 2, n, 4)
                if n + 2 < 12:
                    lower(n % 2, CHUNK0["out1"] + n + 2, 6 if n % 3 == 0 else KC)
            result(KD - 2)
            result(KD - 1)
            norm_scale(4, False, True)
            dve.wait_ge(y_copied, KD)
            for t in (0, 2):
                nc.vector.tensor_scalar(y[:, t, :], y[:, t, :], rcol[:, t:t + 1], None, ALU.mult)\
                    .then_inc(y_scaled_dve, 1)

        @block.tensor
        def _(pe):
            def product(out_, a, b, start, stop):
                nc.tensor.matmul(out_, a[0], b[1], start=start, stop=False)
                nc.tensor.matmul(out_, a[1], b[0], start=False, stop=False)
                return nc.tensor.matmul(out_, a[0], b[0], start=False, stop=stop)

            def w(slot, k, c0, c1):
                return wh[:, slot, k, c0:c1], wl[:, slot, k, c0:c1]

            def by_features(m, b, slot, e, ks, hi, lo, k0=0, first=True, last=True, ready=None):
                if first:
                    ge(pe, tile_free, m - 3)
                for k in range(ks):
                    if ready is not None:
                        pe.wait_ge(ready[0], ready[1] + k0 + k + 1)
                    ins = product(dense[b][:, :], w(slot, k, e * P, (e + 1) * P), (hi[:, k0 + k, :], lo[:, k0 + k, :]),
                                  first and k == 0, last and k == ks - 1)
                if last and e == 0:
                    ins.then_inc(first_done, 1)
                return ins

            def by_tokens(m, b, slot, ready=None):
                for t in range(TT):
                    if t % 2 == 0:
                        ge(pe, tile_free, m + (t // 2 - 3))
                    for k in range(KD):
                        if ready is not None and t == 0:
                            pe.wait_ge(ready[0], ready[1] + k + 1)
                        ins = product(dense[b + t // 2][:, t % 2 * CW:(t % 2 + 1) * CW],
                                      (xh[:, k, t * P:(t + 1) * P], xl[:, k, t * P:(t + 1) * P]), w(slot, k, 0, CW),
                                      k == 0, k == KD - 1)
                    if t == 1:
                        ins.then_inc(first_done, 1)
                return ins

            def chunk_ready(n):
                pe.wait_ge(w_lo, n + 1)

            def norm_sums(norm, rows, columns):
                pe.wait_ge(sq_added, KD * (norm + 1))
                if rows:
                    ins = nc.tensor.matmul(ps_s[0][:, :], ones[:, :], sqsum[:, :], start=True, stop=True)
                if columns:
                    for t in range(TT):
                        ins = nc.tensor.matmul(ps_s[1][:, t:t + 1], sqsum[:, t * P:(t + 1) * P], ones[:, 0:1],
                                               start=True, stop=True)
                ins.then_inc(summed, 1)

            pe.wait_ge(consts, 7)
            pe.wait_ge(nw_loaded, 32)
            nc.tensor.transpose(ps_o[:, 0:32], nw_rows[:, :], ident[0:32, 0:32]).then_inc(nw_turned, 1)
            for k in range(KD):
                if k == 3:
                    pe.wait_ge(nw_ready, 1)
                ge(pe, x_done, k - 3)
                for t in range(TT):
                    if k == 0:
                        pe.wait_ge(x_loaded[t], 16)
                    ins = nc.tensor.transpose(bank[4 + k % 4][:, t * P:(t + 1) * P], x_tok[:, t, k * P:(k + 1) * P],
                                              ident[:, :])
                ins.then_inc(x_turned, 1)

            for c in range(4):
                chunk_ready(c)
                by_tokens(TILE0["v"] + 2 * c, 2 * (c % 2), c % 2, (xl_done, 0) if c == 0 else None).then_inc(w_used, 1)
                if c == 0:
                    pe.wait_ge(x_done, KD)
                    norm_sums(0, True, True)
                    pe.wait_ge(wf_lo, 1)
                    for t in range(TT):
                        for k in range(KD):
                            ins = product(ps_o[:, t * H:(t + 1) * H],
                                          (xh[:, k, t * P:(t + 1) * P], xl[:, k, t * P:(t + 1) * P]),
                                          (wfh[:, k, :], wfl[:, k, :]), k == 0, k == KD - 1)
                    ins.then_inc(f_done, 1)
                if c == 2:
                    pe.wait_ge(logf_done, 1)
                    for t in range(TT):
                        ins = nc.tensor.matmul(ps_t[0:H, t * P:T], fz[:, t * H:(t + 1) * H], tri[:, 0:T - t * P],
                                               start=(t == 0), stop=(t == TT - 1), skip_group_check=True)
                    ins.then_inc(c_summed, 1)

            def qk_part(p, b, part):
                e, q = part // TT, part % TT
                m = p * 2 + (TILE0["qk"] + e)
                if part == 0:
                    chunk_ready(p + CHUNK0["qk"])
                if q == 0:
                    ge(pe, tile_free, m - 3)
                for k in range(2 * q, 2 * q + 2):
                    ins = product(dense[2 * b + e][:, :], w(b, k, e * P, (e + 1) * P), (xh[:, k, :], xl[:, k, :]),
                                  k == 0, k == KD - 1)
                if q == TT - 1:
                    ins.then_inc((first_done, w_used)[e], 1)

            def scores(p, s, b):
                a, i, n = s // TT, s % TT, (s % TT + 1) * P
                S0 = p * STEPS + s
                pe.wait_ge(tile_free, p * 2 + (TILE0["qk"] + 2))
                ge(pe, s_shifted, S0 - 1)
                r = slice(a * HD, (a + 1) * HD)
                nc.tensor.matmul(ps_s[s % 2][:, 0:n], qT[r, b, i * P:(i + 1) * P], kT[r, b, 0:n],
                                 start=True, stop=False, skip_group_check=True)
                nc.tensor.matmul(ps_s[s % 2][:, i * P:n], identr[:, :], mask[:, :],
                                 start=False, stop=True, skip_group_check=True).then_inc(s_done, 1)

            def turn(p, s, after_out=False):
                S0 = p * STEPS + s
                pe.wait_ge(e_done, S0 + 1)
                if after_out:
                    pe.wait_ge(ol_done, p)
                ge(pe, et_ready, S0)
                for j in range(s % TT + 1):
                    ins = nc.tensor.transpose(ps_t[:, j * P:(j + 1) * P], E[:, s % 2, j * P:(j + 1) * P], ident[:, :])
                ins.then_inc(et_done, 1)

            def weigh(p, s):
                a, i = s // TT, s % TT
                S0 = p * STEPS + s
                pe.wait_ge(et_ready, S0 + 1)
                ge(pe, o_ready, p * 2 + a)
                for j in range(i + 1):
                    ins = nc.tensor.matmul(ps_o[:, s * HD:(s + 1) * HD], ET[:, s % 2, j * P:(j + 1) * P],
                                           V[:, j, bass.ds(p * P + a * HD, HD)], start=(j == 0), stop=(j == i))
                ins.then_inc(pv_done, 1)

            def turn_out(p, S1):
                pe.wait_ge(o_ready, p * 2 + 2)
                pe.wait_ge(et_ready, S1)
                for t in range(TT):
                    ins = nc.tensor.transpose(ps_t[:, t * P:(t + 1) * P], o_tok[:, t, :], ident[:, :])
                ins.then_inc(o_turned, 1)

            def attend(p, b, first, last):
                for s in range(STEPS):
                    if s >= 3:
                        weigh(p, s - 3)
                    elif not first:
                        weigh(p - 1, s + STEPS - 3)
                    scores(p, s, b)
                    if s == 5 and not first:
                        turn_out(p - 1, p * STEPS + 4)
                    if not last:
                        qk_part(p + 1, 1 - b, s)
                    if s >= 1:
                        turn(p, s - 1, s == 5 and not first)
                    elif not first:
                        turn(p - 1, STEPS - 1)

            for part in range(STEPS):
                qk_part(0, 0, part)
            attend(0, 0, True, False)
            with Loop(pe, 0, PAIRS // 2 - 1) as i:
                attend(i * 2 + 1, 1, False, False)
                attend(i * 2 + 2, 0, False, False)
            attend(PAIRS - 1, 1, False, True)
            weigh(PAIRS - 1, STEPS - 3)
            turn(PAIRS - 1, STEPS - 1)
            weigh(PAIRS - 1, STEPS - 2)
            weigh(PAIRS - 1, STEPS - 1)
            turn_out(PAIRS - 1, PAIRS * STEPS)

            def residual_pass(name, cuts, hi, lo, ready, i):
                per = 2 * len(cuts)
                n = 0
                for b in range(2):
                    k0 = 0
                    for q, ks in enumerate(cuts):
                        chunk_ready(i * per + (CHUNK0[name] + n))
                        for e in range(2):
                            ins = by_features(i * 4 + (TILE0[name] + 2 * b + e), 2 * b + e, n % 2, e, ks, hi, lo, k0,
                                              q == 0, q == len(cuts) - 1, ready)
                        ins.then_inc(w_used, 1)
                        k0 += ks
                        n += 1

            def ffn_in_chunk(name, j, half, ready=None):
                chunk_ready(j * 2 + (CHUNK0[name] + half))
                for e in range(2):
                    ins = by_features(j * 4 + (TILE0[name] + 2 * half + e), 2 * half + e, half, e, KC, xh, xl,
                                      ready=ready if e == 0 else None)
                ins.then_inc(w_used, 1)

            def ffn_in(name, norm):
                ffn_in_chunk(name, 0, 0, (xl_done, KD * norm))
                norm_sums(norm, True, False)
                ffn_in_chunk(name, 0, 1)
                with Loop(pe, 1, KF // 2) as j:
                    ffn_in_chunk(name, j, 0)
                    ffn_in_chunk(name, j, 1)

            with Loop(pe, 0, 2) as i:
                residual_pass("ao", (8,), oh, ol, (ol_done, 0), i)
            ffn_in("in0", 1)
            with Loop(pe, 0, 2) as i:
                residual_pass("out0", (8, 8, 6), ah, al, (al_done, 0), i)

            def gate_v(c, b, ready=None):
                chunk_ready(c + CHUNK0["sv"])
                by_tokens(c * 2 + TILE0["sv"], 2 * b, b, ready).then_inc(w_used, 1)

            gate_v(0, 0, (xl_done, KD * 2))
            norm_sums(2, True, True)
            gate_v(1, 1)
            with Loop(pe, 1, 4) as i:
                gate_v(i * 2, 0)
                gate_v(i * 2 + 1, 1)
            pe.wait_ge(ws_masked, 1)
            for q in range(4):
                ge(pe, ws_ready, q - 1)
                for g in range(4):
                    ins = nc.tensor.transpose(bank[6 + q % 2][:, g * P:(g + 1) * P], ws[:, 4 * q + g, :], ident[:, :])
                ins.then_inc(ws_turned, 1)

            def gate_u(c, b):
                chunk_ready(c + CHUNK0["su"])
                for e in range(2):
                    ins = by_features(c * 2 + (TILE0["su"] + e), 2 * b + e, b, e, KC, xh, xl)
                ins.then_inc(w_used, 1)

            def mix(c):
                for e in range(2):
                    pe.wait_ge(vn_done, c * 2 + (e + 1))
                    ge(pe, mix_read, c * 2 + (e - 1))
                    for t in range(TT):
                        ins = nc.tensor.matmul(ps_s[e][:, t * P:(t + 1) * P], vt[:, c * 2 + e, t, :],
                                               wsT[:, c * 2 + e, :], start=True, stop=True)
                    ins.then_inc(mixed, 1)

            pe.wait_ge(ws_ready, 4)
            for c in range(8):
                gate_u(c, c % 2)
                mix(c)
            with Loop(pe, 0, 2) as i:
                residual_pass("so", (8, 8), gh, gl, (gl_done, 0), i)
            ffn_in("in1", 3)
            def turn_back(k):
                pe.wait_ge(tile_free, TILE0["out1"] + k + 1)
                ge(pe, y_copied, k - 3)
                for t in range(TT):
                    ins = nc.tensor.transpose(bank[4 + k % 4][:, t * P:(t + 1) * P], xT[:, k, t * P:(t + 1) * P],
                                              ident[:, :])
                ins.then_inc(y_turned, 1)

            for i in range(2):
                for b in range(2):
                    k0 = 0
                    for q, ks in enumerate((8, 8, 6)):
                        n = 6 * i + 3 * b + q
                        chunk_ready(CHUNK0["out1"] + n)
                        for e in range(2):
                            k = 4 * i + 2 * b + e
                            ins = by_features(TILE0["out1"] + k, k % 4, n % 2, e, ks, ah, al, k0, q == 0, q == 2,
                                              (al_done, KF))
                            if e == 1:
                                ins.then_inc(w_used, 1)
                            if q == 1 and 4 * i + 2 * b >= 2:
                                turn_back(4 * i + 2 * b - 2 + e)
                        k0 += ks
            turn_back(KD - 2)
            turn_back(KD - 1)
            norm_sums(4, False, True)


_INPUTS = ["x", "mixer_norm_w", "attn_w_in", "attn_b_f", "attn_w_out", "sgu_w_in", "sgu_ln_g", "sgu_ln_b",
           "sgu_w_s", "sgu_b_s", "sgu_w_out", "ffn_norm_w", "ffn_w_in", "ffn_w_out", "final_norm_w"]


def kernel(**inputs):
    import numpy as np
    import concourse.bacc as bacc
    from concourse.bass_utils import run_bass_kernel_spmd

    nc = bacc.Bacc("TRN2", target_bir_lowering=False, num_devices=1)
    arrays, args = {}, []
    for name in _INPUTS:
        a = np.ascontiguousarray(inputs[name])
        arrays[f"in_{name}"] = a
        args.append(nc.dram_tensor(f"in_{name}", a.shape, mybir.dt.from_np(a.dtype), kind="ExternalInput").ap())
    shape = arrays["in_x"].shape
    args.append(nc.dram_tensor("trunk_out", shape, F32, kind="ExternalOutput").ap())
    trunk_kernel(nc, *args)
    r = run_bass_kernel_spmd(nc, [arrays], core_ids=[0])
    return r.results[0]["trunk_out"]
```

```python
from contextlib import ExitStack

import concourse.bass as bass
from concourse import mybir

F32 = mybir.dt.float32
F32R = mybir.dt.float32r
ALU = mybir.AluOpType
ACT = mybir.ActivationFunctionType

P = 128
T = 512
D = 1024
KD = D // P
TT = T // P
H = 16
HD = D // H
PAIRS = H // 2
STEPS = 2 * TT
G = 16
GW = 2 * D
F = 2816
KF = F // P
KG = GW // P
CW = 256
KC = 8
NORM_EPS = 1e-6
LN_EPS = 1e-5
MASKED = 3.0e38
HALF = (slice(0, HD), slice(HD, P))

PHASES = [("v", 4, 8), ("qk", 8, 16), ("ao", 4, 8), ("in0", 22, 44), ("out0", 12, 8),
          ("sv", 8, 16), ("su", 8, 16), ("so", 8, 8), ("in1", 22, 44), ("out1", 12, 8)]
CHUNK0, TILE0 = {}, {}
_c = _t = 0
for _name, _chunks, _tiles in PHASES:
    CHUNK0[_name], TILE0[_name] = _c, _t
    _c += _chunks
    _t += _tiles
CHUNKS = _c
RES0 = {"ao": 0, "out0": 8, "so": 16, "out1": 24}
NORM_ROW = {0: 0, 1: 16, 2: 8, 3: 24}


class Count:

    def __init__(self, sem):
        self.sem, self.n, self.turn = sem, 0, 0

    def inc(self, ins):
        ins.then_inc(self.sem, 1)
        self.n += 1
        return self.now()

    def now(self):
        return self.turn + self.n


class Loop:

    def __init__(self, eng, first, end, own=()):
        self.eng, self.first, self.end, self.own = eng, first, end, own

    def __enter__(self):
        self.fori = self.eng.Fori(self.first, self.end)
        self.i = self.fori.__enter__()
        self.start = [c.n for c, _ in self.own]
        for c, rise in self.own:
            c.turn = (self.i - self.first) * rise
        return self.i

    def __exit__(self, *a):
        out = self.fori.__exit__(*a)
        for (c, rise), n in zip(self.own, self.start):
            assert a[0] is not None or c.n - n == rise, (c.sem, c.n - n, rise)
            c.n, c.turn = n + rise * (self.end - self.first), 0
        return out


def ge(eng, sem, value):
    if not isinstance(value, int) or value > 0:
        eng.wait_ge(sem, value)


def wait_tile(eng, e, first_done, pair, w_used, chunk):
    if e == 0:
        eng.wait_ge(first_done, pair + 1)
    else:
        eng.wait_ge(w_used, chunk + 1)


def trunk_kernel(nc, x, mixer_norm_w, attn_w_in, attn_b_f, attn_w_out, sgu_w_in, sgu_ln_g, sgu_ln_b,
                 sgu_w_s, sgu_b_s, sgu_w_out, ffn_norm_w, ffn_w_in, ffn_w_out, final_norm_w, out):
    ctx = ExitStack()
    with ctx:
        top = [32 + nc.sbuf_base]

        def at(name, shape, dt, offset):
            return nc.alloc_sbuf_tensor_at(name, shape, dt, offset=offset)

        def place(name, shape, dt=F32):
            size = 4
            for s in shape[1:]:
                size *= s
            t = at(name, shape, dt, top[0])
            top[0] += -(-size // 32) * 32
            return t

        def sem(name):
            return ctx.enter_context(nc.semaphore(name))

        top[0] = -(-top[0] // 32) * 32
        xT = place("xT", [P, KD, T])
        xh_at = top[0]
        xh = place("xh", [P, KD, T], F32R)
        xl_at = top[0]
        xl = place("xl", [P, KD, T], F32R)
        raw = place("raw", [P, 2, KC, CW])
        wh = place("wh", [P, 2, KC, CW], F32R)
        wl = place("wl", [P, 2, KC, CW], F32R)
        tmp = place("tmp", [P, 4, T])
        rms = place("rms", [P, T])
        sq = place("sq", [P, 2, T])
        sqsum = place("sqsum", [P, T])
        ident = place("ident", [P, P])
        ones = place("ones", [P, P])
        nw = place("nw", [P, 32])
        nw_rows = place("nw_rows", [32, P])
        rcol = place("rcol", [P, TT])
        cols = place("cols", [P, 4, TT])
        eps = place("eps", [P, 4])
        lncol = place("lncol", [P, TT, 2])
        rstd = place("rstd", [P, TT])
        xsq = place("xsq", [P, TT])
        base = top[0]

        V = place("V", [P, TT, D])
        o_at = top[0]
        oh = place("oh", [P, KD, T], F32R)
        ol = place("ol", [P, KD, T], F32R)
        x_tok = at("x_tok", [P, TT, D], F32, o_at)
        ol_at, kb = o_at + 4 * KD * T, 4 * KD * P
        wf = at("wf", [P, KD, P], F32, ol_at)
        wfh = at("wfh", [P, KD, P], F32R, ol_at + kb)
        wfl = at("wfl", [P, KD, P], F32R, ol_at + 2 * kb)
        fz = at("fz", [H, T], F32, ol_at + 3 * kb)
        fa = at("fa", [H, T], F32, ol_at + 3 * kb + 4 * T)
        q_both = place("q_both", [P, 2, 2, T], F32R)
        k_both = place("k_both", [P, 2, 2, T], F32R)
        k_low = place("k_low", [P, 2, T], F32R)
        c_bc = place("c_bc", [P, 2, 2, T])
        S = place("S", [P, 2, T])
        E = place("E", [P, 2, T])
        ET = place("ET", [P, 2, T])
        o_tok = place("o_tok", [P, TT, P])
        mask = place("mask", [P, P], F32R)
        identr = place("identr", [P, P], F32R)
        mask32 = place("mask32", [P, P])
        bf = place("bf", [H, 1])
        cT = place("cT", [H, T])
        smin = place("smin", [P, 2])
        rsum = place("rsum", [P, 2, STEPS])
        rinv = place("rinv", [P, 2, TT])
        ends = [top[0]]

        top[0] = base
        ah = place("ah", [P, KF, T], F32R)
        al = place("al", [P, KF, T], F32R)
        ends.append(top[0])

        top[0] = base
        gh_at = top[0]
        gh = place("gh", [P, KG, T], F32R)
        vt = at("vt", [P, G, TT, P], F32, gh_at)
        gl = place("gl", [P, KG, T], F32R)
        wsT = place("wsT", [P, G, P])
        ws = place("ws", [P, G, P])
        gbc = place("gbc", [P, 2, CW])
        bbc = place("bbc", [P, 2, CW])
        sbc = place("sbc", [P, 2, CW])
        stats = place("stats", [P, TT, 8, 6])
        ends.append(top[0])

        y = at("y", [P, TT, D], F32, xh_at)
        fw = at("fw", [P, D], F32, xl_at)
        assert max(ends) <= nc.sbuf_usable_end, (ends, nc.sbuf_usable_end)

        c_dram = nc.dram_tensor("c_scratch", (H, T), F32).ap()

        bank = [ctx.enter_context(nc.psum_tensor(f"bank{b}", [P, T], F32)) for b in range(8)]
        dense = bank[0:4]
        ps_s = bank[4:6]
        ps_t, ps_o = bank[6], bank[7]

        x_loaded = [sem(f"x_loaded{t}") for t in range(TT)]
        nw_loaded = sem("nw_loaded")
        wf_cleared = sem("wf_cleared")
        wf_loaded = sem("wf_loaded")
        ws_loaded = sem("ws_loaded")
        w_loaded = [sem("w_loaded0"), sem("w_loaded1")]
        c_stored = sem("c_stored")
        c_loaded = [sem("c_loaded0"), sem("c_loaded1")]
        ln_loaded = [sem("ln_loaded0"), sem("ln_loaded1")]
        fw_loaded = sem("fw_loaded")
        stored = sem("stored")
        w_hi = sem("w_hi")
        w_lo = sem("w_lo")
        w_used = sem("w_used")
        wf_hi = sem("wf_hi")
        wf_lo = sem("wf_lo")
        first_done = sem("first_done")
        tile_free = sem("tile_free")
        xsq_done = sem("xsq_done")
        x_turned = sem("x_turned")
        nw_turned = sem("nw_turned")
        nw_ready = sem("nw_ready")
        x_done = sem("x_done")
        xh_done = sem("xh_done")
        xl_done = sem("xl_done")
        sq_done = sem("sq_done")
        sq_added = sem("sq_added")
        summed = sem("summed")
        mean_done = sem("mean_done")
        std_done = sem("std_done")
        r_done = sem("r_done")
        spread = sem("spread")
        rms_done = sem("rms_done")
        consts = sem("consts")
        identr_done = sem("identr_done")
        qh_done = sem("qh_done")
        kh_done = sem("kh_done")
        kl_done = sem("kl_done")
        f_done = sem("f_done")
        fz_done = sem("fz_done")
        fe_done = sem("fe_done")
        c_ready = sem("c_ready")
        s_done = sem("s_done")
        s_shifted = sem("s_shifted")
        e_done = sem("e_done")
        et_done = sem("et_done")
        et_ready = sem("et_ready")
        pv_done = sem("pv_done")
        o_ready = sem("o_ready")
        o_turned = sem("o_turned")
        oh_done = sem("oh_done")
        ol_done = sem("ol_done")
        silu_done = sem("silu_done")
        gr_done = sem("gr_done")
        ah_done = sem("ah_done")
        al_done = sem("al_done")
        ws_masked = sem("ws_masked")
        ws_turned = sem("ws_turned")
        ws_ready = sem("ws_ready")
        vg_done = sem("vg_done")
        stats_done = sem("stats_done")
        var_ready = sem("var_ready")
        lnstd_done = sem("lnstd_done")
        vc_done = sem("vc_done")
        vn_done = sem("vn_done")
        u_done = sem("u_done")
        mixed = sem("mixed")
        gated = sem("gated")
        gh_done = sem("gh_done")
        gl_done = sem("gl_done")
        y_turned = sem("y_turned")
        y_copied = sem("y_copied")
        mix_read = sem("mix_read")
        y_scaled_dve = sem("y_scaled_dve")
        y_scaled_act = sem("y_scaled_act")
        dve_step = sem("dve_step")
        pool_step = sem("pool_step")
        passed = {e.engine: sem(f"passed{n}") for n, e in enumerate((nc.scalar, nc.vector, nc.gpsimd))}

        w_view = {
            "v": attn_w_in[0].rearrange("(k p) n -> p k n", p=P),
            "qk": attn_w_in[0].rearrange("(k p) n -> p k n", p=P),
            "ao": attn_w_out[0].rearrange("(k p) n -> p k n", p=P),
            "in0": ffn_w_in[0].rearrange("(k p) n -> p k n", p=P),
            "out0": ffn_w_out[0].rearrange("(k p) n -> p k n", p=P),
            "sv": sgu_w_in[0].rearrange("(k p) n -> p k n", p=P),
            "su": sgu_w_in[0].rearrange("(k p) n -> p k n", p=P),
            "so": sgu_w_out[0].rearrange("(k p) n -> p k n", p=P),
            "in1": ffn_w_in[1].rearrange("(k p) n -> p k n", p=P),
            "out1": ffn_w_out[1].rearrange("(k p) n -> p k n", p=P),
        }

        def apart(eng):
            eng.sem_inc(passed[eng.engine], 1)

        block = ctx.enter_context(nc.Block())

        @block.sync
        def _(sp):
            for t in range(TT):
                sp.dma_start(x_tok[:, t, :], x[0, t * P:(t + 1) * P, :]).then_inc(x_loaded[t], 16)

            def load(slot, n, parts):
                ge(sp, w_lo, n - 1)
                for dst, src in parts:
                    sp.dma_start(dst, src).then_inc(w_loaded[slot], 16)

            def whole(phase, slot, n, col, k0=0, ks=KC):
                h = ks // 2
                load(slot, n, [(raw[:, slot, 0:h, :], w_view[phase][:, k0:k0 + h, bass.ds(col, CW)]),
                               (raw[:, slot, h:ks, :], w_view[phase][:, k0 + h:k0 + ks, bass.ds(col, CW)])])

            for c in range(4):
                whole("v", c % 2, c, 2 * D + c * CW)
                if c == 1:
                    sp.wait_ge(wf_cleared, 1)
                    sp.dma_start(wf[:, :, 0:H], w_view["v"][:, :, 3 * D:3 * D + H]).then_inc(wf_loaded, 16)
                    sp.dma_start(bf[:, :], attn_b_f.rearrange("l (h a) -> (l h) a", a=1)).then_inc(wf_loaded, 16)

            def load_qk(p, slot):
                w = w_view["qk"]
                load(slot, CHUNK0["qk"] + p, [(raw[:, slot, :, 0:P], w[:, :, bass.ds(p * P, P)]),
                                              (raw[:, slot, :, P:CW], w[:, :, bass.ds(p * P + D, P)])])

            def load_c(p, slot):
                ge(sp, s_shifted, STEPS * (p - 1))
                sp.dma_start(c_bc[:, slot, :, :], c_dram[bass.ds(p * 2, 2), :].partition_broadcast(P))\
                    .then_inc(c_loaded[slot], 16)

            load_qk(0, 0)
            load_qk(1, 1)
            sp.wait_ge(c_ready, 1)
            sp.dma_start(c_dram, cT[:, :]).then_inc(c_stored, 16)
            sp.wait_ge(c_stored, 16)
            load_c(0, 0)
            load_c(1, 1)
            with Loop(sp, 0, PAIRS // 2 - 1) as i:
                for b in range(2):
                    load_qk(i * 2 + (b + 2), b)
                    load_c(i * 2 + (b + 2), b)

            def stream(phase, turns, body, first=0):
                with Loop(sp, first, turns) as i:
                    body(i, CHUNK0[phase])

            def columns(phase, col0=0):
                def body(i, n0):
                    for b in range(2):
                        whole(phase, b, i * 2 + (n0 + b), i * (2 * CW) + (col0 + b * CW))
                return body

            def ffn_in(phase):
                def body(i, n0):
                    for b in range(2):
                        whole(phase, b, i * 2 + (n0 + b), i * CW + b * F)
                return body

            def deep(phase, cuts):
                def body(i, n0):
                    n = 0
                    for b in range(2):
                        k0 = 0
                        for ks in cuts:
                            whole(phase, n % 2, i * (2 * len(cuts)) + (n0 + n), i * (2 * CW) + b * CW, k0, ks)
                            k0 += ks
                            n += 1
                return body

            stream("ao", 2, columns("ao"))
            stream("in0", KF // 2, ffn_in("in0"))
            stream("out0", 2, deep("out0", (8, 8, 6)))
            columns("sv", GW)(0, CHUNK0["sv"])
            sp.wait_ge(w_used, CHUNK0["sv"])
            sp.dma_start(ws[:, :, :], sgu_w_s[0].rearrange("g t s -> t g s")).then_inc(ws_loaded, 16)
            stream("sv", 4, columns("sv", GW), 1)

            def load_ln(c, slot):
                ge(sp, gated, 2 * (c - 1))
                for dst, src in ((gbc, sgu_ln_g[0:1, bass.ds(c * CW, CW)]), (bbc, sgu_ln_b[0:1, bass.ds(c * CW, CW)]),
                                 (sbc, sgu_b_s.rearrange("l g t -> l (g t)")[:, bass.ds(c * CW, CW)])):
                    sp.dma_start(dst[:, slot, :], src.partition_broadcast(P)).then_inc(ln_loaded[slot], 16)

            columns("su")(0, CHUNK0["su"])
            for b in range(2):
                load_ln(b, b)
            columns("su")(1, CHUNK0["su"])
            with Loop(sp, 1, 3) as i:
                for b in range(2):
                    whole("su", b, i * 2 + (CHUNK0["su"] + b + 2), i * (2 * CW) + (b + 2) * CW)
                    load_ln(i * 2 + b, b)
            for b in range(2):
                load_ln(6 + b, b)
            stream("so", 2, deep("so", (8, 8)))
            stream("in1", KF // 2, ffn_in("in1"))
            stream("out1", 2, deep("out1", (8, 8, 6)))

            for t in range(TT):
                sp.wait_ge((y_scaled_dve, y_scaled_act)[t % 2], t // 2 + 1)
                sp.dma_start(out[0, t * P:(t + 1) * P, :], y[:, t, :]).then_inc(stored, 16)
            sp.wait_ge(stored, 16 * TT)

        @block.gpsimd
        def _(pool):
            step = Count(pool_step)
            nc.gpsimd.memset(ones[:, :], 1.0).then_inc(consts, 1)
            for e, value in enumerate((NORM_EPS, LN_EPS, 1.0)):
                nc.gpsimd.memset(eps[:, e:e + 1], value).then_inc(consts, 1)
            step.inc(nc.gpsimd.memset(ident[:, :], 0.0))
            step.inc(nc.gpsimd.memset(mask32[:, :], 0.0))
            nc.gpsimd.memset(wf[:, :, :], 0.0).then_inc(wf_cleared, 1)
            pool.wait_ge(pool_step, step.now())
            nc.gpsimd.affine_select(out=ident[:, :], in_=ident[:, :], compare_op=ALU.not_equal, fill=1.0, base=0,
                                    pattern=[[-1, P]], channel_multiplier=1).then_inc(consts, 1)
            nc.gpsimd.affine_select(out=mask32[:, :], in_=mask32[:, :], compare_op=ALU.is_ge, fill=MASKED, base=0,
                                    pattern=[[-1, P]], channel_multiplier=1).then_inc(consts, 1)

            def clear_sum(norm):
                ge(pool, summed, norm - 1)
                step.inc(nc.gpsimd.memset(sqsum[:, :], 0.0))
                pool.wait_ge(pool_step, step.now())

            def add_square(r, slot):
                pool.wait_ge(sq_done, r + 1)
                ge(pool, sq_added, r)
                nc.gpsimd.tensor_tensor(sqsum[:, :], sqsum[:, :], sq[:, slot, :], ALU.add).then_inc(sq_added, 1)

            def sum_pass(name, norm):
                clear_sum(norm)
                for b in range(2):
                    add_square(RES0[name] + b, b)
                with Loop(pool, 1, KD // 2) as i:
                    for b in range(2):
                        add_square(i * 2 + (RES0[name] + b), b)

            def ffn(layer):
                with Loop(pool, 0, KF // 2) as i:
                    for b in range(2):
                        pool.wait_ge(silu_done, i * 2 + (layer * KF + b + 1))
                        nc.gpsimd.tensor_tensor(tmp[:, b, :], tmp[:, b, :], rms[:, :], ALU.mult).then_inc(gr_done, 1)

            sum_pass("ao", 1)
            ffn(0)
            sum_pass("out0", 2)
            pool.wait_ge(ws_loaded, 16)
            nc.gpsimd.affine_select(out=ws[:, :, :], in_=ws[:, :, :], compare_op=ALU.is_ge, fill=0.0, base=0,
                                    pattern=[[0, G], [-1, P]], channel_multiplier=1).then_inc(ws_masked, 1)

            def gains(c, slot):
                pool.wait_ge(vc_done, (c + 1) * TT)
                pool.wait_ge(ln_loaded[slot], c * 24 + (48 - 24 * slot))
                for g in range(2):
                    v = vt[:, bass.ds(c * 2 + g, 1), :, :].rearrange("p a t d -> p (a t) d")
                    gain = gbc[:, slot, g * P:(g + 1) * P].unsqueeze(1).broadcast_to([P, TT, P])
                    bias = bbc[:, slot, g * P:(g + 1) * P].unsqueeze(1).broadcast_to([P, TT, P])
                    step.inc(nc.gpsimd.tensor_tensor(v, v, gain, ALU.mult))
                    pool.wait_ge(pool_step, step.now())
                    apart(pool)
                    nc.gpsimd.tensor_tensor(v, v, bias, ALU.add).then_inc(vn_done, 1)

            with Loop(pool, 0, 4, own=[(step, 4)]) as i:
                for b in range(2):
                    gains(i * 2 + b, b)
            sum_pass("so", 3)
            ffn(1)
            clear_sum(4)
            for k in range(KD - 1):
                add_square(k + RES0["out1"], k % 2)

        @block.scalar
        def _(act):
            def upper(slot, n, ks=KC, parts=1):
                for _ in upper_parts(slot, n, ks, parts):
                    pass

            def upper_parts(slot, n, ks=KC, parts=1):
                act.wait_ge(w_loaded[slot], n * 16 + (32 - 16 * slot))
                ge(act, w_used, n - 1)
                for q in range(parts):
                    k0, k1 = ks * q // parts, ks * (q + 1) // parts
                    ins = nc.scalar.activation(wh[:, slot, k0:k1, :], raw[:, slot, k0:k1, :], ACT.Copy)
                    if q == parts - 1:
                        ins.then_inc(w_hi, 1)
                    yield

            def residual(name, k, slot, norm):
                r = k + RES0[name]
                act.wait_ge(tile_free, k + (TILE0[name] + 1))
                if norm < 4:
                    w = nw[:, bass.ds(k + NORM_ROW[norm], 1)]
                    nc.scalar.activation(xh[:, bass.ds(k, 1), :].rearrange("p a t -> p (a t)"),
                                         xT[:, bass.ds(k, 1), :].rearrange("p a t -> p (a t)"),
                                         ACT.Copy, scale=w).then_inc(xh_done, 1)
                ge(act, sq_added, r - 1)
                apart(act)
                nc.scalar.activation(sq[:, slot, :], xT[:, bass.ds(k, 1), :].rearrange("p a t -> p (a t)"),
                                     ACT.Square).then_inc(sq_done, 1)

            def norm_root(norm):
                act.wait_ge(mean_done, norm + 1)
                nc.scalar.activation(cols[:, 0, :], cols[:, 1, :], ACT.Sqrt).then_inc(std_done, 1)

            def norm_rows(n):
                act.wait_ge(spread, n + 1)
                nc.scalar.activation(rms[:, :], ps_s[0][:, :], ACT.Copy).then_inc(rms_done, 1)

            act.dma_start(nw_rows[0:16, :], mixer_norm_w.rearrange("i (k p) -> (i k) p", p=P)).then_inc(nw_loaded, 16)
            act.dma_start(nw_rows[16:32, :], ffn_norm_w.rearrange("i (k p) -> (i k) p", p=P)).then_inc(nw_loaded, 16)

            act.wait_ge(consts, 6)
            for t in range(TT):
                act.wait_ge(x_loaded[t], 16)
                if t > 0:
                    act.wait_ge(xsq_done, t)
                nc.scalar.activation(tmp[:, 0:2, :].rearrange("p a t -> p (a t)"), x_tok[:, t, :], ACT.Square,
                                     accum_out=xsq[:, t:t + 1]).then_inc(xsq_done, 1)
            norm_root(0)
            upper(0, 0)
            act.wait_ge(nw_ready, 1)
            for k in range(KD):
                act.wait_ge(x_turned, k + 1)
                nc.scalar.activation(xh[:, k, :], bank[k][:, :], ACT.Copy, scale=nw[:, k:k + 1]).then_inc(xh_done, 1)
            for k in range(1, KD):
                if k == 2:
                    upper(1, 1)
                act.wait_ge(xl_done, k + 1)
                nc.scalar.activation(xT[:, k, :], bank[k][:, :], ACT.Copy).then_inc(x_done, 1)
            norm_rows(0)
            act.wait_ge(wf_loaded, 32)
            nc.scalar.activation(wfh[:, :, :], wf[:, :, :], ACT.Copy).then_inc(wf_hi, 1)
            nc.scalar.activation(mask[:, :], mask32[:, :], ACT.Copy).then_inc(identr_done, 1)
            nc.scalar.activation(identr[:, :], ident[:, :], ACT.Copy).then_inc(identr_done, 1)
            upper(0, 2)
            upper(1, 3)
            act.wait_ge(fz_done, 1)
            nc.scalar.activation(fa[:, :], fa[:, :], ACT.Exp, scale=-1.0).then_inc(fe_done, 1)
            act.wait_ge(fe_done, 1)
            nc.scalar.activation(fa[:, :], fa[:, :], ACT.Ln, bias=eps[0:H, 2:3]).then_inc(fe_done, 1)
            upper(0, 4)
            upper(1, 5)

            def exps(p, s, b):
                i, n = s % TT, (s % TT + 1) * P
                S0 = p * STEPS + s
                act.wait_ge(s_shifted, S0 + 1)
                ge(act, et_done, S0 - 1)
                nc.scalar.activation(E[:, s % 2, 0:n], S[:, s % 2, 0:n], ACT.Exp, bias=smin[:, s % 2:s % 2 + 1],
                                     scale=-1.0, accum_out=rsum[:, b, s:s + 1]).then_inc(e_done, 1)

            def copy_turned(p, s):
                n = (s % TT + 1) * P
                S0 = p * STEPS + s
                act.wait_ge(et_done, S0 + 1)
                ge(act, pv_done, S0 - 1)
                nc.scalar.activation(ET[:, s % 2, 0:n], ps_t[:, 0:n], ACT.Copy).then_inc(et_ready, 1)

            def out_upper(p):
                act.wait_ge(o_turned, p + 1)
                nc.scalar.activation(oh[:, bass.ds(p, 1), :].rearrange("p a t -> p (a t)"), ps_t[:, :], ACT.Copy)\
                    .then_inc(oh_done, 1)

            def queries_upper(p, b):
                act.wait_ge(tile_free, p * 2 + (TILE0["qk"] + 1))
                for a in range(2):
                    r = HALF[a]
                    ins = nc.scalar.activation(q_both[r, b, a, :], tmp[r, 0, :], ACT.Copy)
                ins.then_inc(qh_done, 1)

            def keys_upper(p, a, b):
                act.wait_ge(tile_free, p * 2 + (TILE0["qk"] + 2))
                for half in HALF:
                    ins = nc.scalar.activation(k_both[half, b, a, :], tmp[HALF[a], 1, :], ACT.Copy)
                ins.then_inc(kh_done, 1)

            def attend(p, b, first, last):
                split = upper_parts(b, p + (CHUNK0["qk"] + 2), KC, 3)
                for s in range(STEPS):
                    if s == 5 and not first:
                        out_upper(p - 1)
                    if s == STEPS - 1 and not last:
                        keys_upper(p + 1, 0, 1 - b)
                    exps(p, s, b)
                    if s >= 1:
                        copy_turned(p, s - 1)
                    elif not first:
                        copy_turned(p - 1, STEPS - 1)
                    next(split, None)
                    if s == 3 and not last:
                        queries_upper(p + 1, 1 - b)
                if not last:
                    keys_upper(p + 1, 1, 1 - b)
                if last:
                    copy_turned(p, STEPS - 1)
                    out_upper(p)

            queries_upper(0, 0)
            for a in range(2):
                keys_upper(0, a, 0)
            attend(0, 0, True, False)
            with Loop(act, 0, PAIRS // 2 - 1) as i:
                attend(i * 2 + 1, 1, False, False)
                attend(i * 2 + 2, 0, False, False)
            attend(PAIRS - 1, 1, False, True)

            def residual_pass(name, norm, cuts):
                per = 2 * len(cuts)

                def half(i):
                    for n in range(per):
                        if n % len(cuts) == len(cuts) - 1:
                            if name == "ao":
                                upper(n % 2, i * per + (CHUNK0[name] + n + 2))
                            for e in range(2):
                                k = i * 4 + (n // len(cuts) * 2 + e)
                                residual(name, k, e, norm)
                        size = cuts[(n + 2) % len(cuts)] if n + 2 < per else KC
                        if name != "ao":
                            upper(n % 2, i * per + (CHUNK0[name] + n + 2), size)

                if RES0[name] == 0:
                    half(0)
                    half(1)
                else:
                    with Loop(act, 0, 2) as i:
                        half(i)

            def ffn_in(name, layer, norm):
                norm_root(norm)
                norm_rows(norm)
                with Loop(act, 0, KF // 2) as j:
                    for e in range(2):
                        act.wait_ge(tile_free, j * 4 + (TILE0[name] + e + 1))
                        nc.scalar.activation(tmp[:, e, :], tmp[:, e, :], ACT.Silu).then_inc(silu_done, 1)
                    upper(0, j * 2 + (CHUNK0[name] + 2))
                    for e in range(2):
                        act.wait_ge(tile_free, j * 4 + (TILE0[name] + e + 3))
                        nc.scalar.activation(ah[:, bass.ds(j * 2 + e, 1), :].rearrange("p a t -> p (a t)"),
                                             tmp[:, 2 + e, :], ACT.Copy).then_inc(ah_done, 1)
                    upper(1, j * 2 + (CHUNK0[name] + 3))

            residual_pass("ao", 1, (8,))
            ffn_in("in0", 0, 1)
            residual_pass("out0", 2, (8, 8, 6))

            norm_root(2)
            with Loop(act, 0, 4) as i:
                for b in range(2):
                    for t in range(TT):
                        act.wait_ge(tile_free, i * 4 + (TILE0["sv"] + 2 * b + t // 2 + 1))
                        v = vt[:, bass.ds(i * 4 + 2 * b, 2), t, :]
                        nc.scalar.activation(v, v, ACT.Gelu).then_inc(vg_done, 1)
                    upper(b, i * 2 + (CHUNK0["sv"] + b + 2))
            norm_rows(2)
            act.wait_ge(var_ready, 1)
            nc.scalar.activation(cols[:, 0, :], lncol[:, :, 1], ACT.Sqrt, bias=eps[:, 1:2]).then_inc(lnstd_done, 1)

            with Loop(act, 0, 4) as i:
                for b in range(2):
                    for e in range(2):
                        act.wait_ge(tile_free, i * 4 + (TILE0["su"] + 2 * b + e + 1))
                        nc.scalar.activation(tmp[:, e, :], tmp[:, e, :], ACT.Gelu).then_inc(u_done, 1)
                    upper(b, i * 2 + (CHUNK0["su"] + b + 2))
                    for e in range(2):
                        act.wait_ge(gated, i * 4 + (2 * b + e + 1))
                        nc.scalar.activation(gh[:, bass.ds(i * 4 + (2 * b + e), 1), :].rearrange("p a t -> p (a t)"),
                                             tmp[:, 2 + e, :], ACT.Copy).then_inc(gh_done, 1)
            residual_pass("so", 3, (8, 8))
            ffn_in("in1", 1, 3)

            for n in range(12):
                if n == 11:
                    nc.scalar.activation(cols[0:1, 2, 0:1], eps[0:1, 2:3], ACT.Sqrt)
                if n % 3 == 2:
                    for e in range(2):
                        k = n // 3 * 2 + e
                        residual("out1", k, e, 4)
                if n + 2 < 12:
                    upper(n % 2, CHUNK0["out1"] + n + 2, 6 if n % 3 == 0 else KC)
                if n == 0:
                    act.wait_ge(w_used, CHUNK0["out1"])
                    act.dma_start(fw[:, :], final_norm_w.rearrange("(a d) -> a d", a=1).partition_broadcast(P))\
                        .then_inc(fw_loaded, 16)
            norm_root(4)
            act.wait_ge(r_done, 5)
            act.wait_ge(y_copied, KD)
            for t in (1, 3):
                nc.scalar.activation(y[:, t, :], y[:, t, :], ACT.Copy, scale=rcol[:, t:t + 1]).then_inc(y_scaled_act, 1)

        @block.vector
        def _(dve):
            step = Count(dve_step)

            def chained(ins):
                dve.wait_ge(dve_step, step.inc(ins))

            def tile_of(buf, k):
                return buf[:, bass.ds(k, 1), :].rearrange("p a t -> p (a t)")

            def lower_parts(slot, n, ks=KC, parts=1):
                dve.wait_ge(w_hi, n + 1)
                ge(dve, w_used, n - 1)
                for q in range(parts):
                    k0, k1 = ks * q // parts, ks * (q + 1) // parts
                    ins = nc.vector.tensor_tensor(wl[:, slot, k0:k1, :], raw[:, slot, k0:k1, :],
                                                  wh[:, slot, k0:k1, :].bitcast(F32), ALU.subtract)
                    if q == parts - 1:
                        ins.then_inc(w_lo, 1)
                    yield

            def lower(slot, n, ks=KC):
                for _ in lower_parts(slot, n, ks):
                    pass

            def input_lower(r, k, norm):
                dve.wait_ge(xh_done, r + (KD + 1))
                nc.vector.scalar_tensor_tensor(out=tile_of(xl, k), in0=tile_of(xT, k),
                                               scalar=nw[:, bass.ds(k + NORM_ROW[norm], 1)],
                                               in1=tile_of(xh, k).bitcast(F32), op0=ALU.mult,
                                               op1=ALU.subtract).then_inc(xl_done, 1)

            def newton(out_, mean, root, r, t):
                chained(nc.vector.reciprocal(r, root))
                chained(nc.vector.tensor_tensor(t, r, r, ALU.mult))
                chained(nc.vector.tensor_tensor(t, t, mean, ALU.mult))
                chained(nc.vector.tensor_scalar(t, t, -0.5, 1.5, ALU.mult, ALU.add))
                return nc.vector.tensor_tensor(out_, r, t, ALU.mult)

            def norm_scale(norm):
                if norm > 0:
                    dve.wait_ge(summed, norm)
                else:
                    dve.wait_ge(xsq_done, TT)
                ins = nc.vector.tensor_scalar(cols[:, 1, :], ps_s[1][:, 0:TT] if norm > 0 else xsq[:, :], 1.0 / D,
                                              NORM_EPS, ALU.mult, ALU.add)
                if norm == 4:
                    chained(ins)
                    dve.wait_ge(summed, 5)
                    ins = nc.vector.scalar_tensor_tensor(out=cols[:, 1, :], in0=ps_s[0][:, 0:TT], scalar=1.0 / D,
                                                         in1=cols[:, 1, :], op0=ALU.mult, op1=ALU.add)
                ins.then_inc(mean_done, 1)
                dve.wait_ge(std_done, norm + 1)
                newton(rcol[:, :], cols[:, 1, :], cols[:, 0, :], cols[:, 2, :], cols[:, 3, :]).then_inc(r_done, 1)
                dve.wait_ge(r_done, norm + 1)

            dve.wait_ge(consts, 6)
            dve.wait_ge(nw_turned, 1)
            nc.vector.tensor_copy(nw[:, :], bank[0][:, 0:32]).then_inc(nw_ready, 1)
            dve.wait_ge(nw_ready, 1)
            norm_scale(0)
            lower(0, 0)
            for k in range(KD):
                dve.wait_ge(xh_done, k + 1)
                if k == 0:
                    nc.vector.tensor_copy(xT[:, k, :], bank[k][:, :])
                nc.vector.scalar_tensor_tensor(out=xl[:, k, :], in0=bank[k][:, :], scalar=nw[:, k:k + 1],
                                               in1=xh[:, k, :].bitcast(F32), op0=ALU.mult,
                                               op1=ALU.subtract).then_inc(xl_done, 1)
            lower(1, 1)
            dve.wait_ge(wf_hi, 1)
            nc.vector.tensor_tensor(wfl[:, :, :], wf[:, :, :], wfh[:, :, :].bitcast(F32), ALU.subtract)\
                .then_inc(wf_lo, 1)

            def values(c, m):
                for t in range(TT):
                    if t % 2 == 0:
                        wait_tile(dve, t // 2, first_done, m // 2, w_used, c)
                    ins = nc.vector.tensor_scalar(V[:, t, c * CW:(c + 1) * CW],
                                                  dense[(m + t // 2) % 4][:, t % 2 * CW:(t % 2 + 1) * CW],
                                                  rcol[:, t:t + 1], None, ALU.mult)
                    if t % 2 == 1:
                        ins.then_inc(tile_free, 1)

            ones_row = ones[0:H, 0:1].broadcast_to([H, T])
            for c in range(4):
                values(c, TILE0["v"] + 2 * c)
                lower(c % 2, c + 2)
                if c == 1:
                    dve.wait_ge(f_done, 1)
                    dve.wait_ge(rms_done, 1)
                    chained(nc.vector.tensor_tensor(fz[:, :], ps_o[0:H, :], rms[0:H, :], ALU.mult))
                    chained(nc.vector.tensor_scalar(fz[:, :], fz[:, :], bf[:, 0:1], None, ALU.add))
                    nc.vector.scalar_tensor_tensor(out=fa[:, :], in0=fz[:, :], scalar=-1.0, in1=fz[:, :],
                                                   op0=ALU.mult, op1=ALU.max).then_inc(fz_done, 1)
                if c == 2:
                    dve.wait_ge(fe_done, 2)
                    chained(nc.vector.scalar_tensor_tensor(out=fz[:, :], in0=fz[:, :], scalar=0.0, in1=fa[:, :],
                                                           op0=ALU.min, op1=ALU.subtract))
                    nc.vector.tensor_tensor_scan(cT[:, :], ones_row, fz[:, :], 0.0, ALU.mult, ALU.add)\
                        .then_inc(c_ready, 1)

            def queries(p, b):
                dve.wait_ge(first_done, p + (TILE0["qk"] // 2 + 1))
                nc.vector.scalar_tensor_tensor(out=tmp[:, 0, :], in0=dense[2 * b][:, :], scalar=-(HD ** -0.5),
                                               in1=rms[:, :], op0=ALU.mult, op1=ALU.mult)\
                    .then_inc(tile_free, 1)

            def keys(p, b):
                dve.wait_ge(w_used, p + (CHUNK0["qk"] + 1))
                nc.vector.tensor_tensor(tmp[:, 1, :], dense[2 * b + 1][:, :], rms[:, :], ALU.mult)\
                    .then_inc(tile_free, 1)

            def queries_lower(p, b):
                dve.wait_ge(qh_done, p + 1)
                for a in range(2):
                    r, other = HALF[a], HALF[1 - a]
                    nc.vector.tensor_tensor(q_both[other, b, a, :], tmp[r, 0, :], q_both[r, b, a, :].bitcast(F32),
                                            ALU.subtract)

            def keys_lower(p, a, b):
                dve.wait_ge(kh_done, p * 2 + (a + 1))
                r = HALF[a]
                nc.vector.tensor_tensor(k_low[r, b, :], tmp[r, 1, :], k_both[r, b, a, :].bitcast(F32),
                                        ALU.subtract).then_inc(kl_done, 1)

            def shift(p, s, b):
                i, n = s % TT, (s % TT + 1) * P
                S0 = p * STEPS + s
                dve.wait_ge(s_done, S0 + 1)
                if s == 0:
                    dve.wait_ge(c_loaded[b], p * 8 + (16 - 8 * b))
                ge(dve, e_done, S0 - 1)
                apart(dve)
                nc.vector.tensor_tensor_reduce(S[:, s % 2, 0:n], ps_s[s % 2][:, 0:n], c_bc[:, b, s // TT, 0:n],
                                               1.0, 3.4e38, ALU.add, ALU.min, smin[:, s % 2:s % 2 + 1])\
                    .then_inc(s_shifted, 1)

            def normalised(p, a, b):
                dve.wait_ge(e_done, p * STEPS + (a + 1) * TT)
                chained(nc.vector.reciprocal(rinv[:, b, :], rsum[:, b, a * TT:(a + 1) * TT]))
                dve.wait_ge(pv_done, p * STEPS + (a + 1) * TT)
                nc.vector.tensor_tensor(o_tok[:, :, a * HD:(a + 1) * HD],
                                        ps_o[:, a * TT * HD:(a + 1) * TT * HD].rearrange("p (i d) -> p i d", d=HD),
                                        rinv[:, b, :].unsqueeze(2).broadcast_to([P, TT, HD]), ALU.mult)\
                    .then_inc(o_ready, 1)

            def out_lower(p):
                dve.wait_ge(oh_done, p + 1)
                nc.vector.tensor_tensor(tile_of(ol, p), ps_t[:, :], tile_of(oh, p).bitcast(F32), ALU.subtract)\
                    .then_inc(ol_done, 1)

            def attend(p, b, first, last):
                split = lower_parts(b, p + (CHUNK0["qk"] + 2), KC, TT)
                for s in range(STEPS):
                    if s == 5 and not first:
                        out_lower(p - 1)
                    shift(p, s, b)
                    if s == 2 and not first:
                        normalised(p - 1, 1, 1 - b)
                    if s == 3 and not last:
                        queries(p + 1, 1 - b)
                    if s == 6:
                        normalised(p, 0, b)
                    if 3 <= s < 3 + TT:
                        next(split)
                    if s == 4 and not last:
                        queries_lower(p + 1, 1 - b)
                    if s == 6 and not last:
                        keys(p + 1, 1 - b)
                if not last:
                    for a in range(2):
                        keys_lower(p + 1, a, 1 - b)
                else:
                    normalised(p, 1, b)
                    out_lower(p)

            queries(0, 0)
            keys(0, 0)
            queries_lower(0, 0)
            for a in range(2):
                keys_lower(0, a, 0)
            attend(0, 0, True, False)
            with Loop(dve, 0, PAIRS // 2 - 1, own=[(step, 4)]) as i:
                attend(i * 2 + 1, 1, False, False)
                attend(i * 2 + 2, 0, False, False)
            attend(PAIRS - 1, 1, False, True)

            def gained(name, k, e, bank_, pair, chunk):
                wait_tile(dve, e, first_done, pair + TILE0[name] // 2, w_used, chunk + CHUNK0[name])
                nc.vector.tensor_tensor(tile_of(xT, k), tile_of(xT, k), dense[bank_][:, :], ALU.add)\
                    .then_inc(tile_free, 1)

            def residual_pass(name, norm, cuts):
                per = 2 * len(cuts)
                with Loop(dve, 0, 2) as i:
                    for n in range(per):
                        if n % len(cuts) == len(cuts) - 1:
                            for e in range(2):
                                t = n // len(cuts) * 2 + e
                                gained(name, i * 4 + t, e, t, i * 2 + t // 2, i * per + n)
                                if name != "ao":
                                    input_lower(i * 4 + (t + RES0[name]), i * 4 + t, norm)
                        size = cuts[(n + 2) % len(cuts)] if n + 2 < per else KC
                        lower(n % 2, i * per + (CHUNK0[name] + n + 2), size)
                        if name == "ao":
                            for k in range(2 * n, 2 * n + 2):
                                input_lower(i * 4 + (k + RES0[name]), i * 4 + k, norm)

            def ffn_in(name, layer, norm):
                norm_scale(norm)
                dve.wait_ge(rms_done, norm + 1)
                with Loop(dve, 0, KF // 2) as j:
                    for e in range(2):
                        wait_tile(dve, e, first_done, j * 2 + TILE0[name] // 2, w_used, j * 2 + CHUNK0[name])
                        nc.vector.tensor_tensor(tmp[:, e, :], dense[e][:, :], rms[:, :], ALU.mult)\
                            .then_inc(tile_free, 1)
                    lower(0, j * 2 + (CHUNK0[name] + 2))
                    for e in range(2):
                        wait_tile(dve, e, first_done, j * 2 + (TILE0[name] // 2 + 1), w_used,
                                  j * 2 + (CHUNK0[name] + 1))
                        dve.wait_ge(gr_done, j * 2 + (layer * KF + e + 1))
                        nc.vector.tensor_tensor(tmp[:, 2 + e, :], dense[2 + e][:, :], tmp[:, e, :], ALU.mult)\
                            .then_inc(tile_free, 1)
                    for e in range(2):
                        dve.wait_ge(ah_done, j * 2 + (layer * KF + e + 1))
                        nc.vector.tensor_tensor(tile_of(al, j * 2 + e), tmp[:, 2 + e, :],
                                                tile_of(ah, j * 2 + e).bitcast(F32), ALU.subtract)\
                            .then_inc(al_done, 1)
                    lower(1, j * 2 + (CHUNK0[name] + 3))

            residual_pass("ao", 1, (8,))
            ffn_in("in0", 0, 1)
            residual_pass("out0", 2, (8, 8, 6))

            norm_scale(2)

            def gate_v(i, turned):
                for b in range(2):
                    for t in range(TT):
                        if t % 2 == 0:
                            wait_tile(dve, t // 2, first_done, i * 2 + (TILE0["sv"] // 2 + b), w_used,
                                      i * 2 + (CHUNK0["sv"] + b))
                        ins = nc.vector.tensor_scalar(
                            vt[:, bass.ds(i * 4 + 2 * b, 2), t, :],
                            dense[2 * b + t // 2][:, t % 2 * CW:(t % 2 + 1) * CW].rearrange("p (g d) -> p g d", d=P),
                            rcol[:, t:t + 1], None, ALU.mult)
                        if t % 2 == 1:
                            ins.then_inc(tile_free, 1)
                    for t in range(TT):
                        dve.wait_ge(vg_done, i * (2 * TT) + (b * TT + t + 1))
                        ins = nc.vector.bn_stats(stats[:, t, bass.ds(i * 2 + b, 1), :].rearrange("p a s -> p (a s)"),
                                                 vt[:, bass.ds(i * 4 + 2 * b, 2), t, :])
                    ins.then_inc(stats_done, 1)
                    lower(b, i * 2 + (CHUNK0["sv"] + b + 2))
                    if turned:
                        for q in range(2 * b, 2 * b + 2):
                            dve.wait_ge(ws_turned, q + 1)
                            nc.vector.tensor_copy(wsT[:, 4 * q:4 * q + 4, :],
                                                  bank[6 + q % 2].rearrange("p (g t) -> p g t", t=P))\
                                .then_inc(ws_ready, 1)

            with Loop(dve, 0, 3) as i:
                gate_v(i, False)
            gate_v(3, True)
            dve.wait_ge(stats_done, 8)
            for t in range(TT):
                ins = nc.vector.bn_aggr(lncol[:, t, :], stats[:, t, :, :].rearrange("p c s -> p (c s)"))
            ins.then_inc(var_ready, 1)
            dve.wait_ge(var_ready, 1)
            chained(nc.vector.tensor_scalar(cols[:, 1, :], lncol[:, :, 1], LN_EPS, None, ALU.add))
            dve.wait_ge(lnstd_done, 1)
            chained(newton(rstd[:, :], cols[:, 1, :], cols[:, 0, :], cols[:, 2, :], cols[:, 3, :]))

            def centred(c):
                for t in range(TT):
                    v = vt[:, bass.ds(c * 2, 2), t, :]
                    nc.vector.tensor_scalar(v, v, lncol[:, t, 0:1], rstd[:, t:t + 1], ALU.subtract, ALU.mult)\
                        .then_inc(vc_done, 1)

            def gate(c, b, ahead):
                for e in range(2):
                    wait_tile(dve, e, first_done, c + TILE0["su"] // 2, w_used, c + CHUNK0["su"])
                    nc.vector.tensor_tensor(tmp[:, e, :], dense[2 * b + e][:, :], rms[:, :], ALU.mult)\
                        .then_inc(tile_free, 1)
                if ahead:
                    centred(c + 1)
                lower(b, c + (CHUNK0["su"] + 2))
                dve.wait_ge(ln_loaded[b], c * 24 + (48 - 24 * b))
                ge(dve, gl_done, c * 2)
                for e in range(2):
                    dve.wait_ge(mixed, c * 2 + (e + 1))
                    t = tmp[:, 2 + e, :].rearrange("p (c t) -> p c t", t=P)
                    nc.vector.tensor_tensor(t, ps_s[e].rearrange("p (c t) -> p c t", t=P),
                                            sbc[:, b, e * P:(e + 1) * P].unsqueeze(1).broadcast_to([P, TT, P]),
                                            ALU.add).then_inc(mix_read, 1)
                for e in range(2):
                    dve.wait_ge(mix_read, c * 2 + (e + 1))
                    dve.wait_ge(u_done, c * 2 + (e + 1))
                    nc.vector.tensor_tensor(tmp[:, 2 + e, :], tmp[:, 2 + e, :], tmp[:, e, :], ALU.mult)\
                        .then_inc(gated, 1)
                for e in range(2):
                    dve.wait_ge(gh_done, c * 2 + (e + 1))
                    nc.vector.tensor_tensor(tile_of(gl, c * 2 + e), tmp[:, 2 + e, :],
                                            tile_of(gh, c * 2 + e).bitcast(F32), ALU.subtract).then_inc(gl_done, 1)

            centred(0)
            gate(0, 0, True)
            gate(1, 1, True)
            with Loop(dve, 1, 3) as i:
                gate(i * 2, 0, True)
                gate(i * 2 + 1, 1, True)
            gate(6, 0, True)
            gate(7, 1, False)
            residual_pass("so", 3, (8, 8))
            ffn_in("in1", 1, 3)

            def result(k):
                dve.wait_ge(y_turned, k + 1)
                nc.vector.tensor_tensor(y[:, :, k * P:(k + 1) * P], bank[4 + k % 4].rearrange("p (t d) -> p t d", d=P),
                                        fw[:, k * P:(k + 1) * P].unsqueeze(1).broadcast_to([P, TT, P]), ALU.mult)\
                    .then_inc(y_copied, 1)

            for n in range(12):
                if n % 3 == 2:
                    if n == 5:
                        dve.wait_ge(fw_loaded, 16)
                    if n > 2:
                        for e in range(2):
                            result(n // 3 * 2 - 2 + e)
                    for e in range(2):
                        k = n // 3 * 2 + e
                        gained("out1", k, e, k % 4, k // 2, n)
                if n + 2 < 12:
                    lower(n % 2, CHUNK0["out1"] + n + 2, 6 if n % 3 == 0 else KC)
            result(KD - 2)
            result(KD - 1)
            norm_scale(4)
            dve.wait_ge(y_copied, KD)
            for t in (0, 2):
                nc.vector.tensor_scalar(y[:, t, :], y[:, t, :], rcol[:, t:t + 1], None, ALU.mult)\
                    .then_inc(y_scaled_dve, 1)

        @block.tensor
        def _(pe):
            def product(out_, a, b, start, stop):
                nc.tensor.matmul(out_, a[0], b[1], start=start, stop=False)
                nc.tensor.matmul(out_, a[1], b[0], start=False, stop=False)
                return nc.tensor.matmul(out_, a[0], b[0], start=False, stop=stop)

            def w(slot, k, c0, c1):
                return wh[:, slot, k, c0:c1], wl[:, slot, k, c0:c1]

            def by_features(m, b, slot, e, ks, hi, lo, k0=0, first=True, last=True, ready=None):
                if first:
                    ge(pe, tile_free, m - 3)
                for k in range(ks):
                    if ready is not None:
                        pe.wait_ge(ready[0], ready[1] + k0 + k + 1)
                    ins = product(dense[b][:, :], w(slot, k, e * P, (e + 1) * P), (hi[:, k0 + k, :], lo[:, k0 + k, :]),
                                  first and k == 0, last and k == ks - 1)
                if last and e == 0:
                    ins.then_inc(first_done, 1)
                return ins

            def by_tokens(m, b, slot, ready=None, second=None):
                for t in range(TT):
                    if second and t == 2:
                        pe.wait_ge(*second)
                    if t % 2 == 0:
                        ge(pe, tile_free, m + (t // 2 - 3))
                    for k in range(KD):
                        if ready is not None and t == 0:
                            pe.wait_ge(ready[0], ready[1] + k + 1)
                        ins = product(dense[b + t // 2][:, t % 2 * CW:(t % 2 + 1) * CW],
                                      (xh[:, k, t * P:(t + 1) * P], xl[:, k, t * P:(t + 1) * P]), w(slot, k, 0, CW),
                                      k == 0, k == KD - 1)
                    if t == 1:
                        ins.then_inc(first_done, 1)
                return ins

            def chunk_ready(n):
                pe.wait_ge(w_lo, n + 1)

            def norm_sums(norm):
                pe.wait_ge(sq_added, KD * norm)
                for t in range(TT):
                    ins = nc.tensor.matmul(ps_s[1][:, t:t + 1], sqsum[:, t * P:(t + 1) * P], ones[:, 0:1],
                                           start=True, stop=True)
                ins.then_inc(summed, 1)

            def norm_spread(norm):
                pe.wait_ge(r_done, norm + 1)
                for t in range(TT):
                    ins = nc.tensor.matmul(ps_s[0][:, t * P:(t + 1) * P], rcol[:, t:t + 1].broadcast_to([P, P]),
                                           ident[:, :], start=True, stop=True)
                ins.then_inc(spread, 1)

            pe.wait_ge(consts, 6)
            pe.wait_ge(nw_loaded, 32)
            nc.tensor.transpose(bank[0][:, 0:32], nw_rows[:, :], ident[0:32, 0:32]).then_inc(nw_turned, 1)
            pe.wait_ge(nw_ready, 1)
            for t in range(TT):
                pe.wait_ge(x_loaded[t], 16)
                for k in range(KD):
                    ins = nc.tensor.transpose(bank[k][:, t * P:(t + 1) * P], x_tok[:, t, k * P:(k + 1) * P],
                                              ident[:, :])
                    if t == TT - 1:
                        ins.then_inc(x_turned, 1)

            for c in range(4):
                chunk_ready(c)
                by_tokens(TILE0["v"] + 2 * c, 2 * (c % 2), c % 2, (xl_done, 0) if c == 0 else None,
                          (x_done, 1) if c == 0 else None).then_inc(w_used, 1)
                if c == 0:
                    pe.wait_ge(x_done, KD - 1)
                    norm_spread(0)
                if c == 1:
                    pe.wait_ge(wf_lo, 1)
                    for k in range(KD):
                        ins = product(ps_o[:, :], (wfh[:, k, :], wfl[:, k, :]), (xh[:, k, :], xl[:, k, :]),
                                      k == 0, k == KD - 1)
                    ins.then_inc(f_done, 1)

            def qk_part(p, b, part):
                e, q = part // TT, part % TT
                m = p * 2 + (TILE0["qk"] + e)
                if part == 0:
                    chunk_ready(p + CHUNK0["qk"])
                if q == 0:
                    ge(pe, tile_free, m - 3)
                for k in range(2 * q, 2 * q + 2):
                    ins = product(dense[2 * b + e][:, :], w(b, k, e * P, (e + 1) * P), (xh[:, k, :], xl[:, k, :]),
                                  k == 0, k == KD - 1)
                if q == TT - 1:
                    ins.then_inc((first_done, w_used)[e], 1)

            def scores(p, s, b):
                a, i, n = s // TT, s % TT, (s % TT + 1) * P
                S0 = p * STEPS + s
                if i == 0:
                    pe.wait_ge(kl_done, p * 2 + (a + 1))
                ge(pe, s_shifted, S0 - 1)
                r = slice(a * HD, (a + 1) * HD)
                nc.tensor.matmul(ps_s[s % 2][:, 0:n], q_both[:, b, a, i * P:(i + 1) * P], k_both[:, b, a, 0:n],
                                 start=True, stop=False, skip_group_check=True)
                nc.tensor.matmul(ps_s[s % 2][:, 0:n], q_both[r, b, a, i * P:(i + 1) * P], k_low[r, b, 0:n],
                                 start=False, stop=False, skip_group_check=True)
                nc.tensor.matmul(ps_s[s % 2][:, i * P:n], identr[:, :], mask[:, :],
                                 start=False, stop=True, skip_group_check=True).then_inc(s_done, 1)

            def turn(p, s, after_out=False):
                S0 = p * STEPS + s
                pe.wait_ge(e_done, S0 + 1)
                if after_out:
                    pe.wait_ge(ol_done, p)
                ge(pe, et_ready, S0)
                for j in range(s % TT + 1):
                    ins = nc.tensor.transpose(ps_t[:, j * P:(j + 1) * P], E[:, s % 2, j * P:(j + 1) * P], ident[:, :])
                ins.then_inc(et_done, 1)

            def weigh(p, s):
                a, i = s // TT, s % TT
                S0 = p * STEPS + s
                pe.wait_ge(et_ready, S0 + 1)
                ge(pe, o_ready, p * 2 + a)
                for j in range(i + 1):
                    ins = nc.tensor.matmul(ps_o[:, s * HD:(s + 1) * HD], ET[:, s % 2, j * P:(j + 1) * P],
                                           V[:, j, bass.ds(p * P + a * HD, HD)], start=(j == 0), stop=(j == i))
                ins.then_inc(pv_done, 1)

            def turn_out(p, S1):
                pe.wait_ge(o_ready, p * 2 + 2)
                pe.wait_ge(et_ready, S1)
                for t in range(TT):
                    ins = nc.tensor.transpose(ps_t[:, t * P:(t + 1) * P], o_tok[:, t, :], ident[:, :])
                ins.then_inc(o_turned, 1)

            def attend(p, b, first, last):
                for s in range(STEPS):
                    if s >= 3:
                        weigh(p, s - 3)
                    elif not first:
                        weigh(p - 1, s + STEPS - 3)
                    if s == 5 and not first:
                        turn_out(p - 1, p * STEPS + 4)
                    if s == 0 and not last:
                        qk_part(p + 1, 1 - b, 0)
                    scores(p, s, b)
                    if not last and s < STEPS - 1:
                        qk_part(p + 1, 1 - b, s + 1)
                    elif last and s < STEPS - 1:
                        out_part(0, 2 * s, 2 * s + 2)
                    if s >= 1:
                        turn(p, s - 1, s == 5 and not first)
                    elif not first:
                        turn(p - 1, STEPS - 1)

            def out_part(c, first, end):
                n = CHUNK0["ao"] + c
                for u in range(first, end):
                    k, e = u // 2, u % 2
                    if u == 0:
                        chunk_ready(n)
                    if k == 0:
                        ge(pe, tile_free, TILE0["ao"] + 2 * c + e - 3)
                    pe.wait_ge(ol_done, k + 1)
                    ins = product(dense[2 * c + e][:, :], w(c, k, e * P, (e + 1) * P), (oh[:, k, :], ol[:, k, :]),
                                  k == 0, k == KD - 1)
                    if k == KD - 1:
                        ins.then_inc((first_done, w_used)[e], 1)

            for part in range(STEPS):
                qk_part(0, 0, part)
            attend(0, 0, True, False)
            with Loop(pe, 0, PAIRS // 2 - 1) as i:
                attend(i * 2 + 1, 1, False, False)
                attend(i * 2 + 2, 0, False, False)
            attend(PAIRS - 1, 1, False, True)
            weigh(PAIRS - 1, STEPS - 3)
            turn(PAIRS - 1, STEPS - 1)
            out_part(1, 0, 2)
            weigh(PAIRS - 1, STEPS - 2)
            out_part(1, 2, 4)
            weigh(PAIRS - 1, STEPS - 1)
            out_part(1, 4, 6)
            turn_out(PAIRS - 1, PAIRS * STEPS)
            out_part(1, 6, 8)
            out_part(0, 14, 16)
            out_part(1, 8, 16)

            def residual_pass(name, cuts, hi, lo, ready, i, after_first=None):
                per = 2 * len(cuts)
                n = 0
                for b in range(2):
                    k0 = 0
                    for q, ks in enumerate(cuts):
                        chunk_ready(i * per + (CHUNK0[name] + n))
                        for e in range(2):
                            ins = by_features(i * 4 + (TILE0[name] + 2 * b + e), 2 * b + e, n % 2, e, ks, hi, lo, k0,
                                              q == 0, q == len(cuts) - 1, ready)
                        ins.then_inc(w_used, 1)
                        if n == 0 and after_first:
                            after_first()
                        k0 += ks
                        n += 1

            def ffn_in_chunk(name, j, half, ready=None, between=None):
                chunk_ready(j * 2 + (CHUNK0[name] + half))
                for e in range(2):
                    if e == 1 and between:
                        between()
                    ins = by_features(j * 4 + (TILE0[name] + 2 * half + e), 2 * half + e, half, e, KC, xh, xl,
                                      ready=ready if e == 0 else None)
                ins.then_inc(w_used, 1)

            def ffn_in(name, norm):
                ffn_in_chunk(name, 0, 0, (xl_done, KD * norm), lambda: norm_sums(norm))
                norm_spread(norm)
                ffn_in_chunk(name, 0, 1)
                with Loop(pe, 1, KF // 2) as j:
                    ffn_in_chunk(name, j, 0)
                    ffn_in_chunk(name, j, 1)

            residual_pass("ao", (8,), oh, ol, None, 1)
            ffn_in("in0", 1)
            with Loop(pe, 0, 2) as i:
                residual_pass("out0", (8, 8, 6), ah, al, (al_done, 0), i)

            def gate_v(c, b, ready=None):
                chunk_ready(c + CHUNK0["sv"])
                by_tokens(c * 2 + TILE0["sv"], 2 * b, b, ready).then_inc(w_used, 1)

            gate_v(0, 0, (xl_done, KD * 2))
            norm_sums(2)
            gate_v(1, 1)
            norm_spread(2)
            with Loop(pe, 1, 3) as i:
                gate_v(i * 2, 0)
                gate_v(i * 2 + 1, 1)
            pe.wait_ge(ws_masked, 1)
            for c in (6, 7):
                gate_v(c, c - 6)
                for q in range(2 * (c - 6), 2 * (c - 6) + 2):
                    ge(pe, ws_ready, q - 1)
                    for g in range(4):
                        ins = nc.tensor.transpose(bank[6 + q % 2][:, g * P:(g + 1) * P], ws[:, 4 * q + g, :],
                                                  ident[:, :])
                    ins.then_inc(ws_turned, 1)

            def gate_u(c, b):
                chunk_ready(c + CHUNK0["su"])
                for e in range(2):
                    ins = by_features(c * 2 + (TILE0["su"] + e), 2 * b + e, b, e, KC, xh, xl)
                ins.then_inc(w_used, 1)

            def mix(c):
                for e in range(2):
                    pe.wait_ge(vn_done, c * 2 + (e + 1))
                    ge(pe, mix_read, c * 2 + (e - 1))
                    for t in range(TT):
                        ins = nc.tensor.matmul(ps_s[e][:, t * P:(t + 1) * P], vt[:, c * 2 + e, t, :],
                                               wsT[:, c * 2 + e, :], start=True, stop=True)
                    ins.then_inc(mixed, 1)

            gate_u(0, 0)
            pe.wait_ge(ws_ready, 4)
            for c in range(1, 8):
                gate_u(c, c % 2)
                mix(c - 1)
            residual_pass("so", (8, 8), gh, gl, (gl_done, 0), 0, lambda: mix(7))
            residual_pass("so", (8, 8), gh, gl, (gl_done, 0), 1)
            ffn_in("in1", 3)
            def turn_back(k):
                pe.wait_ge(tile_free, TILE0["out1"] + k + 1)
                ge(pe, y_copied, k - 3)
                for t in range(TT):
                    ins = nc.tensor.transpose(bank[4 + k % 4][:, t * P:(t + 1) * P], xT[:, k, t * P:(t + 1) * P],
                                              ident[:, :])
                ins.then_inc(y_turned, 1)

            for i in range(2):
                for b in range(2):
                    k0 = 0
                    for q, ks in enumerate((8, 8, 6)):
                        n = 6 * i + 3 * b + q
                        chunk_ready(CHUNK0["out1"] + n)
                        for e in range(2):
                            k = 4 * i + 2 * b + e
                            ins = by_features(TILE0["out1"] + k, k % 4, n % 2, e, ks, ah, al, k0, q == 0, q == 2,
                                              (al_done, KF))
                            if e == 1:
                                ins.then_inc(w_used, 1)
                            if q == 1 and 4 * i + 2 * b >= 2:
                                turn_back(4 * i + 2 * b - 2 + e)
                        k0 += ks
            turn_back(KD - 2)
            pe.wait_ge(y_copied, KD - 2)
            for last in range(2):
                pe.wait_ge((sq_added, sq_done)[last], 4 * KD - (1, 0)[last])
                for t in range(TT):
                    squares = (sqsum[:, t * P:(t + 1) * P], sq[:, 1, t * P:(t + 1) * P])[last]
                    ins = nc.tensor.matmul(ps_s[1 - last][:, t:t + 1], squares, ones[:, 0:1], start=True, stop=True)
                ins.then_inc(summed, 1)
                if last == 0:
                    turn_back(KD - 1)


_INPUTS = ["x", "mixer_norm_w", "attn_w_in", "attn_b_f", "attn_w_out", "sgu_w_in", "sgu_ln_g", "sgu_ln_b",
           "sgu_w_s", "sgu_b_s", "sgu_w_out", "ffn_norm_w", "ffn_w_in", "ffn_w_out", "final_norm_w"]


def kernel(**inputs):
    import numpy as np
    import concourse.bacc as bacc
    from concourse.bass_utils import run_bass_kernel_spmd

    nc = bacc.Bacc("TRN2", target_bir_lowering=False, num_devices=1)
    arrays, args = {}, []
    for name in _INPUTS:
        a = np.ascontiguousarray(inputs[name])
        arrays[f"in_{name}"] = a
        args.append(nc.dram_tensor(f"in_{name}", a.shape, mybir.dt.from_np(a.dtype), kind="ExternalInput").ap())
    shape = arrays["in_x"].shape
    args.append(nc.dram_tensor("trunk_out", shape, F32, kind="ExternalOutput").ap())
    trunk_kernel(nc, *args)
    r = run_bass_kernel_spmd(nc, [arrays], core_ids=[0])
    return r.results[0]["trunk_out"]
```

```python
from contextlib import ExitStack

import concourse.bass as bass
from concourse import mybir

F32 = mybir.dt.float32
F32R = mybir.dt.float32r
ALU = mybir.AluOpType
ACT = mybir.ActivationFunctionType

P = 128
T = 512
D = 1024
KD = D // P
TT = T // P
H = 16
HD = D // H
PAIRS = H // 2
STEPS = 2 * TT
G = 16
GW = 2 * D
F = 2816
KF = F // P
KG = GW // P
CW = 256
KC = 8
NORM_EPS = 1e-6
LN_EPS = 1e-5
MASKED = 3.0e38
LOW = 32
HALF = (slice(0, HD), slice(HD, P))

PHASES = [("v", 4, 8), ("qk", 8, 16), ("ao", 4, 8), ("in0", 22, 44), ("out0", 12, 8),
          ("sv", 8, 16), ("su", 8, 16), ("so", 8, 8), ("in1", 22, 44), ("out1", 12, 8)]
CHUNK0, TILE0 = {}, {}
_c = _t = 0
for _name, _chunks, _tiles in PHASES:
    CHUNK0[_name], TILE0[_name] = _c, _t
    _c += _chunks
    _t += _tiles
CHUNKS = _c
RES0 = {"ao": 0, "out0": 8, "so": 16, "out1": 24}
NORM_ROW = {0: 0, 1: 16, 2: 8, 3: 24}


class Count:

    def __init__(self, sem):
        self.sem, self.n, self.turn = sem, 0, 0

    def inc(self, ins):
        ins.then_inc(self.sem, 1)
        self.n += 1
        return self.now()

    def now(self):
        return self.turn + self.n


class Loop:

    def __init__(self, eng, first, end, own=()):
        self.eng, self.first, self.end, self.own = eng, first, end, own

    def __enter__(self):
        self.fori = self.eng.Fori(self.first, self.end)
        self.i = self.fori.__enter__()
        self.start = [c.n for c, _ in self.own]
        for c, rise in self.own:
            c.turn = (self.i - self.first) * rise
        return self.i

    def __exit__(self, *a):
        out = self.fori.__exit__(*a)
        for (c, rise), n in zip(self.own, self.start):
            assert a[0] is not None or c.n - n == rise, (c.sem, c.n - n, rise)
            c.n, c.turn = n + rise * (self.end - self.first), 0
        return out


def ge(eng, sem, value):
    if not isinstance(value, int) or value > 0:
        eng.wait_ge(sem, value)


def wait_tile(eng, e, first_done, pair, w_used, chunk):
    if e == 0:
        eng.wait_ge(first_done, pair + 1)
    else:
        eng.wait_ge(w_used, chunk + 1)


def trunk_kernel(nc, x, mixer_norm_w, attn_w_in, attn_b_f, attn_w_out, sgu_w_in, sgu_ln_g, sgu_ln_b,
                 sgu_w_s, sgu_b_s, sgu_w_out, ffn_norm_w, ffn_w_in, ffn_w_out, final_norm_w, out):
    ctx = ExitStack()
    with ctx:
        top = [32 + nc.sbuf_base]

        def at(name, shape, dt, offset):
            return nc.alloc_sbuf_tensor_at(name, shape, dt, offset=offset)

        def place(name, shape, dt=F32):
            size = 4
            for s in shape[1:]:
                size *= s
            t = at(name, shape, dt, top[0])
            top[0] += -(-size // 32) * 32
            return t

        def sem(name):
            return ctx.enter_context(nc.semaphore(name))

        top[0] = -(-top[0] // 32) * 32
        xT = place("xT", [P, KD, T])
        xh_at = top[0]
        xh = place("xh", [P, KD, T], F32R)
        xl_at = top[0]
        xl = place("xl", [P, KD, T], F32R)
        raw = place("raw", [P, 2, KC, CW])
        wh = place("wh", [P, 2, KC, CW], F32R)
        wl = place("wl", [P, 2, KC, CW], F32R)
        tmp = place("tmp", [P, 4, T])
        rms = place("rms", [P, T])
        sq = place("sq", [P, 2, T])
        sqsum = place("sqsum", [P, T])
        ident = place("ident", [P, P])
        ones = place("ones", [P, P])
        nw = place("nw", [P, 32])
        nw_rows = place("nw_rows", [32, P])
        rcol = place("rcol", [P, TT])
        cols = place("cols", [P, 4, TT])
        bias = place("bias", [P, 2])
        lncol = place("lncol", [P, TT, 2])
        rstd = place("rstd", [P, TT])
        xsq = place("xsq", [P, TT])
        base = top[0]

        V = place("V", [P, TT, D])
        o_at = top[0]
        oh = place("oh", [P, KD, T], F32R)
        ol = place("ol", [P, KD, T], F32R)
        x_tok = at("x_tok", [P, TT, D], F32, o_at)
        ol_at, kb = o_at + 4 * KD * T, 4 * KD * P
        wf = at("wf", [P, KD, P], F32, ol_at)
        wfs = at("wfs", [P, KD, P], F32R, ol_at + kb)
        fz = at("fz", [H, T], F32, ol_at + 2 * kb)
        fa = at("fa", [H, T], F32, ol_at + 2 * kb + 4 * T)
        q_both = place("q_both", [P, 2, 2, T], F32R)
        k_both = place("k_both", [P, 2, 2, T], F32R)
        k_low = place("k_low", [P, 2, T], F32R)
        c_bc = place("c_bc", [P, 2, 2, T])
        S = place("S", [P, 2, T])
        E = place("E", [P, 2, T])
        ET = place("ET", [P, 2, T])
        o_tok = place("o_tok", [P, TT, P])
        mask = place("mask", [P, P], F32R)
        identr = place("identr", [P, P], F32R)
        mask32 = place("mask32", [P, P])
        bf = place("bf", [H, 1])
        cT = place("cT", [H, T])
        smin = place("smin", [P, 2])
        rsum = place("rsum", [P, 2, STEPS])
        rinv = place("rinv", [P, 2, TT])
        ends = [top[0]]

        top[0] = base
        ah = place("ah", [P, KF, T], F32R)
        al = place("al", [P, KF, T], F32R)
        ends.append(top[0])

        top[0] = base
        gh_at = top[0]
        gh = place("gh", [P, KG, T], F32R)
        vt = at("vt", [P, G, TT, P], F32, gh_at)
        gl = place("gl", [P, KG, T], F32R)
        wsT = place("wsT", [P, G, P])
        ws = place("ws", [P, G, P])
        gbc = place("gbc", [P, 2, CW])
        bbc = place("bbc", [P, 2, CW])
        sbc = place("sbc", [P, 2, CW])
        stats = place("stats", [P, TT, 8, 6])
        ends.append(top[0])

        y = at("y", [P, TT, D], F32, xh_at)
        fw = at("fw", [P, D], F32, xl_at)
        assert max(ends) <= nc.sbuf_usable_end, (ends, nc.sbuf_usable_end)

        c_dram = nc.dram_tensor("c_scratch", (H, T), F32).ap()

        bank = [ctx.enter_context(nc.psum_tensor(f"bank{b}", [P, T], F32)) for b in range(8)]
        dense = bank[0:4]
        ps_s = bank[4:6]
        ps_t, ps_o = bank[6], bank[7]

        x_loaded = [sem(f"x_loaded{t}") for t in range(TT)]
        nw_loaded = sem("nw_loaded")
        wf_cleared = sem("wf_cleared")
        wf_loaded = sem("wf_loaded")
        ws_loaded = sem("ws_loaded")
        w_loaded = [sem("w_loaded0"), sem("w_loaded1")]
        c_stored = sem("c_stored")
        c_loaded = [sem("c_loaded0"), sem("c_loaded1")]
        ln_loaded = [sem("ln_loaded0"), sem("ln_loaded1")]
        fw_loaded = sem("fw_loaded")
        stored = sem("stored")
        w_hi = sem("w_hi")
        w_lo = sem("w_lo")
        w_used = sem("w_used")
        wf_hi = sem("wf_hi")
        wf_lo = sem("wf_lo")
        first_done = sem("first_done")
        tile_free = sem("tile_free")
        xsq_done = sem("xsq_done")
        x_turned = sem("x_turned")
        x_weighed = sem("x_weighed")
        nw_turned = sem("nw_turned")
        nw_ready = sem("nw_ready")
        x_done = sem("x_done")
        xh_done = sem("xh_done")
        xl_done = sem("xl_done")
        sq_done = sem("sq_done")
        sq_added = sem("sq_added")
        summed = sem("summed")
        mean_done = sem("mean_done")
        std_done = sem("std_done")
        r_done = sem("r_done")
        spread = sem("spread")
        rms_done = sem("rms_done")
        consts = sem("consts")
        mask_ready = sem("mask_ready")
        qh_done = sem("qh_done")
        kh_done = sem("kh_done")
        kl_done = sem("kl_done")
        f_done = sem("f_done")
        fz_done = sem("fz_done")
        fe_done = sem("fe_done")
        c_ready = sem("c_ready")
        s_done = sem("s_done")
        s_shifted = sem("s_shifted")
        e_done = sem("e_done")
        et_done = sem("et_done")
        et_ready = sem("et_ready")
        pv_done = sem("pv_done")
        o_ready = sem("o_ready")
        o_turned = sem("o_turned")
        oh_done = sem("oh_done")
        ol_done = sem("ol_done")
        silu_done = sem("silu_done")
        gr_done = sem("gr_done")
        ah_done = sem("ah_done")
        al_done = sem("al_done")
        ws_masked = sem("ws_masked")
        ws_turned = sem("ws_turned")
        ws_ready = sem("ws_ready")
        vg_done = sem("vg_done")
        stats_done = sem("stats_done")
        var_ready = sem("var_ready")
        lnstd_done = sem("lnstd_done")
        vc_done = sem("vc_done")
        vn_done = sem("vn_done")
        u_done = sem("u_done")
        mixed = sem("mixed")
        mix_read = sem("mix_read")
        gated = sem("gated")
        gh_done = sem("gh_done")
        gl_done = sem("gl_done")
        half_done = sem("half_done")
        y_turned = sem("y_turned")
        y_copied = sem("y_copied")
        y_scaled_dve = sem("y_scaled_dve")
        y_scaled_act = sem("y_scaled_act")
        dve_step = sem("dve_step")
        pool_step = sem("pool_step")
        passed = {e.engine: sem(f"passed{n}") for n, e in enumerate((nc.scalar, nc.vector, nc.gpsimd))}

        w_view = {
            "v": attn_w_in[0].rearrange("(k p) n -> p k n", p=P),
            "qk": attn_w_in[0].rearrange("(k p) n -> p k n", p=P),
            "ao": attn_w_out[0].rearrange("(k p) n -> p k n", p=P),
            "in0": ffn_w_in[0].rearrange("(k p) n -> p k n", p=P),
            "out0": ffn_w_out[0].rearrange("(k p) n -> p k n", p=P),
            "sv": sgu_w_in[0].rearrange("(k p) n -> p k n", p=P),
            "su": sgu_w_in[0].rearrange("(k p) n -> p k n", p=P),
            "so": sgu_w_out[0].rearrange("(k p) n -> p k n", p=P),
            "in1": ffn_w_in[1].rearrange("(k p) n -> p k n", p=P),
            "out1": ffn_w_out[1].rearrange("(k p) n -> p k n", p=P),
        }

        def apart(eng):
            eng.sem_inc(passed[eng.engine], 1)

        def last_bank(h, e):
            return bank[(2, 0)[h] + e]

        def turned_half(h, e):
            return bank[(6, 4)[h] + e]

        def x_half(buf, t, h):
            return buf[:, 4 * h:4 * h + 4, t * P:(t + 1) * P]

        def turned(t, h):
            return bank[4 + 2 * (t % 2) + h].rearrange("p (k t) -> p k t", t=P)

        def weighed(t, h):
            return tmp[:, 2 * (t % 2) + h, :].rearrange("p (k t) -> p k t", t=P)

        block = ctx.enter_context(nc.Block())

        @block.sync
        def _(sp):
            def load_x(t):
                sp.dma_start(x_tok[:, t, :], x[0, t * P:(t + 1) * P, :]).then_inc(x_loaded[t], 16)

            load_x(0)

            def load(slot, n, parts):
                ge(sp, w_lo, n - 1)
                for dst, src in parts:
                    sp.dma_start(dst, src).then_inc(w_loaded[slot], 16)

            def whole(phase, slot, n, col, k0=0, ks=KC):
                h = ks // 2
                load(slot, n, [(raw[:, slot, 0:h, :], w_view[phase][:, k0:k0 + h, bass.ds(col, CW)]),
                               (raw[:, slot, h:ks, :], w_view[phase][:, k0 + h:k0 + ks, bass.ds(col, CW)])])

            for c in range(4):
                whole("v", c % 2, c, 2 * D + c * CW)
                if c == 0:
                    for t in range(1, TT):
                        load_x(t)
                if c == 1:
                    sp.wait_ge(wf_cleared, 1)
                    sp.dma_start(wf[:, :, 0:H], w_view["v"][:, :, 3 * D:3 * D + H]).then_inc(wf_loaded, 16)
                    sp.dma_start(bf[:, :], attn_b_f.rearrange("l (h a) -> (l h) a", a=1)).then_inc(wf_loaded, 16)

            def load_qk(p, slot):
                w = w_view["qk"]
                load(slot, CHUNK0["qk"] + p, [(raw[:, slot, :, 0:P], w[:, :, bass.ds(p * P, P)]),
                                              (raw[:, slot, :, P:CW], w[:, :, bass.ds(p * P + D, P)])])

            def load_c(p, slot):
                ge(sp, s_shifted, STEPS * (p - 1))
                sp.dma_start(c_bc[:, slot, :, :], c_dram[bass.ds(p * 2, 2), :].partition_broadcast(P))\
                    .then_inc(c_loaded[slot], 16)

            load_qk(0, 0)
            load_qk(1, 1)
            sp.wait_ge(c_ready, 1)
            sp.dma_start(c_dram, cT[:, :]).then_inc(c_stored, 16)
            sp.wait_ge(c_stored, 16)
            load_c(0, 0)
            load_c(1, 1)
            with Loop(sp, 0, PAIRS // 2 - 1) as i:
                for b in range(2):
                    load_qk(i * 2 + (b + 2), b)
                    load_c(i * 2 + (b + 2), b)

            def stream(phase, turns, body, first=0):
                with Loop(sp, first, turns) as i:
                    body(i, CHUNK0[phase])

            def columns(phase, col0=0):
                def body(i, n0):
                    for b in range(2):
                        whole(phase, b, i * 2 + (n0 + b), i * (2 * CW) + (col0 + b * CW))
                return body

            def ffn_in(phase):
                def body(i, n0):
                    for b in range(2):
                        whole(phase, b, i * 2 + (n0 + b), i * CW + b * F)
                return body

            def deep(phase, cuts):
                def body(i, n0):
                    n = 0
                    for b in range(2):
                        k0 = 0
                        for ks in cuts:
                            whole(phase, n % 2, i * (2 * len(cuts)) + (n0 + n), i * (2 * CW) + b * CW, k0, ks)
                            k0 += ks
                            n += 1
                return body

            stream("ao", 2, columns("ao"))
            stream("in0", KF // 2, ffn_in("in0"))
            stream("out0", 2, deep("out0", (8, 8, 6)))
            columns("sv", GW)(0, CHUNK0["sv"])
            sp.wait_ge(w_used, CHUNK0["sv"])
            sp.dma_start(ws[:, :, :], sgu_w_s[0].rearrange("g t s -> t g s")).then_inc(ws_loaded, 16)
            stream("sv", 4, columns("sv", GW), 1)

            def load_ln(c, slot):
                ge(sp, gated, 2 * (c - 1))
                for dst, src in ((gbc, sgu_ln_g[0:1, bass.ds(c * CW, CW)]), (bbc, sgu_ln_b[0:1, bass.ds(c * CW, CW)]),
                                 (sbc, sgu_b_s.rearrange("l g t -> l (g t)")[:, bass.ds(c * CW, CW)])):
                    sp.dma_start(dst[:, slot, :], src.partition_broadcast(P)).then_inc(ln_loaded[slot], 16)

            columns("su")(0, CHUNK0["su"])
            for b in range(2):
                load_ln(b, b)
            columns("su")(1, CHUNK0["su"])
            with Loop(sp, 1, 3) as i:
                for b in range(2):
                    whole("su", b, i * 2 + (CHUNK0["su"] + b + 2), i * (2 * CW) + (b + 2) * CW)
                    load_ln(i * 2 + b, b)
            for b in range(2):
                load_ln(6 + b, b)
            stream("so", 2, deep("so", (8, 8)))
            stream("in1", KF // 2, ffn_in("in1"))
            stream("out1", 2, deep("out1", (8, 8, 6)))

            for t in range(TT):
                sp.wait_ge((y_scaled_dve, y_scaled_act)[t % 2], t // 2 + 1)
                sp.dma_start(out[0, t * P:(t + 1) * P, :], y[:, t, :]).then_inc(stored, 16)
            sp.wait_ge(stored, 16 * TT)

        @block.gpsimd
        def _(pool):
            step = Count(pool_step)
            nc.gpsimd.memset(ones[:, :], 1.0).then_inc(consts, 1)
            for e, value in enumerate((LN_EPS, 1.0)):
                nc.gpsimd.memset(bias[:, e:e + 1], value).then_inc(consts, 1)
            step.inc(nc.gpsimd.memset(ident[:, :], 0.0))
            step.inc(nc.gpsimd.memset(mask32[:, :], 0.0))
            nc.gpsimd.memset(wf[:, :, :], 0.0).then_inc(wf_cleared, 1)
            pool.wait_ge(pool_step, step.now())
            nc.gpsimd.affine_select(out=ident[:, :], in_=ident[:, :], compare_op=ALU.not_equal, fill=1.0, base=0,
                                    pattern=[[-1, P]], channel_multiplier=1).then_inc(consts, 1)
            nc.gpsimd.affine_select(out=mask32[:, :], in_=mask32[:, :], compare_op=ALU.is_ge, fill=MASKED, base=0,
                                    pattern=[[-1, P]], channel_multiplier=1).then_inc(consts, 1)

            def clear_sum(norm):
                ge(pool, summed, norm - 1)
                step.inc(nc.gpsimd.memset(sqsum[:, :], 0.0))
                pool.wait_ge(pool_step, step.now())

            def add_square(r, slot):
                pool.wait_ge(sq_done, r + 1)
                ge(pool, sq_added, r)
                nc.gpsimd.tensor_tensor(sqsum[:, :], sqsum[:, :], sq[:, slot, :], ALU.add).then_inc(sq_added, 1)

            def sum_pass(name, norm):
                clear_sum(norm)
                for b in range(2):
                    add_square(RES0[name] + b, b)
                with Loop(pool, 1, KD // 2) as i:
                    for b in range(2):
                        add_square(i * 2 + (RES0[name] + b), b)

            def ffn(layer):
                with Loop(pool, 0, KF // 2) as i:
                    for b in range(2):
                        pool.wait_ge(silu_done, i * 2 + (layer * KF + b + 1))
                        nc.gpsimd.tensor_tensor(tmp[:, b, :], tmp[:, b, :], rms[:, :], ALU.mult).then_inc(gr_done, 1)

            sum_pass("ao", 1)
            ffn(0)
            sum_pass("out0", 2)
            pool.wait_ge(ws_loaded, 16)
            nc.gpsimd.affine_select(out=ws[:, :, :], in_=ws[:, :, :], compare_op=ALU.is_ge, fill=0.0, base=0,
                                    pattern=[[0, G], [-1, P]], channel_multiplier=1).then_inc(ws_masked, 1)

            def gains(c, slot):
                pool.wait_ge(vc_done, (c + 1) * TT)
                pool.wait_ge(ln_loaded[slot], c * 24 + (48 - 24 * slot))
                for g in range(2):
                    v = vt[:, bass.ds(c * 2 + g, 1), :, :].rearrange("p a t d -> p (a t) d")
                    gain = gbc[:, slot, g * P:(g + 1) * P].unsqueeze(1).broadcast_to([P, TT, P])
                    shift = bbc[:, slot, g * P:(g + 1) * P].unsqueeze(1).broadcast_to([P, TT, P])
                    step.inc(nc.gpsimd.tensor_tensor(v, v, gain, ALU.mult))
                    pool.wait_ge(pool_step, step.now())
                    apart(pool)
                    nc.gpsimd.tensor_tensor(v, v, shift, ALU.add).then_inc(vn_done, 1)

            with Loop(pool, 0, 4, own=[(step, 4)]) as i:
                for b in range(2):
                    gains(i * 2 + b, b)
            sum_pass("so", 3)
            ffn(1)
            clear_sum(4)
            for k in range(KD - 2):
                add_square(k + RES0["out1"], k % 2)

        @block.scalar
        def _(act):
            def upper(slot, n, ks=KC, parts=1):
                for _ in upper_parts(slot, n, ks, parts):
                    pass

            def upper_parts(slot, n, ks=KC, parts=1):
                act.wait_ge(w_loaded[slot], n * 16 + (32 - 16 * slot))
                ge(act, w_used, n - 1)
                for q in range(parts):
                    k0, k1 = ks * q // parts, ks * (q + 1) // parts
                    ins = nc.scalar.activation(wh[:, slot, k0:k1, :], raw[:, slot, k0:k1, :], ACT.Copy)
                    if q == parts - 1:
                        ins.then_inc(w_hi, 1)
                    yield

            def residual(name, k, slot, norm):
                r = k + RES0[name]
                act.wait_ge(tile_free, k + (TILE0[name] + 1))
                if norm < 4:
                    w = nw[:, bass.ds(k + NORM_ROW[norm], 1)]
                    nc.scalar.activation(xh[:, bass.ds(k, 1), :].rearrange("p a t -> p (a t)"),
                                         xT[:, bass.ds(k, 1), :].rearrange("p a t -> p (a t)"),
                                         ACT.Copy, scale=w).then_inc(xh_done, 1)
                ge(act, sq_added, r - 1)
                apart(act)
                nc.scalar.activation(sq[:, slot, :], xT[:, bass.ds(k, 1), :].rearrange("p a t -> p (a t)"),
                                     ACT.Square).then_inc(sq_done, 1)

            def norm_root(norm):
                act.wait_ge(mean_done, norm + 1)
                nc.scalar.activation(cols[:, 0, :], cols[:, 1, :], ACT.Sqrt).then_inc(std_done, 1)

            def norm_rows(n):
                act.wait_ge(spread, n + 1)
                nc.scalar.activation(rms[:, :], ps_s[0][:, :], ACT.Copy).then_inc(rms_done, 1)

            act.dma_start(nw_rows[0:16, :], mixer_norm_w.rearrange("i (k p) -> (i k) p", p=P)).then_inc(nw_loaded, 16)
            act.dma_start(nw_rows[16:32, :], ffn_norm_w.rearrange("i (k p) -> (i k) p", p=P)).then_inc(nw_loaded, 16)

            act.wait_ge(consts, 5)
            nc.scalar.activation(cols[0:1, 2, 0:1], bias[0:1, 1:2], ACT.Copy)

            def input_upper(t):
                for h in range(2):
                    act.wait_ge(x_weighed, 2 * t + h + 1)
                    nc.scalar.activation(x_half(xh, t, h), weighed(t, h), ACT.Copy).then_inc(xh_done, 1)

            def stream_tile(t):
                for h in range(2):
                    nc.scalar.activation(x_half(xT, t, h), turned(t, h), ACT.Copy).then_inc(x_done, 1)

            input_upper(0)
            upper(0, 0)
            stream_tile(0)
            for t in range(1, TT):
                input_upper(t)
                stream_tile(t)
            upper(1, 1)
            for t in range(TT):
                ge(act, xsq_done, t)
                nc.scalar.activation(E[:, :, :].rearrange("p a t -> p (a t)"), x_tok[:, t, :], ACT.Square,
                                     accum_out=xsq[:, t:t + 1]).then_inc(xsq_done, 1)
            norm_root(0)
            act.wait_ge(wf_loaded, 32)
            nc.scalar.activation(wfs[:, :, :], wf[:, :, :], ACT.Copy).then_inc(wf_hi, 1)
            nc.scalar.activation(mask[:, :], mask32[:, :], ACT.Copy).then_inc(mask_ready, 1)
            nc.scalar.activation(identr[:, :], ident[:, :], ACT.Copy).then_inc(mask_ready, 1)
            upper(0, 2)
            norm_rows(0)
            upper(1, 3)
            act.wait_ge(fz_done, 1)
            nc.scalar.activation(fa[:, :], fa[:, :], ACT.Exp, scale=-1.0).then_inc(fe_done, 1)
            act.wait_ge(fe_done, 1)
            nc.scalar.activation(fa[:, :], fa[:, :], ACT.Ln, bias=bias[0:H, 1:2]).then_inc(fe_done, 1)
            upper(0, 4)
            upper(1, 5)

            def exps(p, s, b):
                i, n = s % TT, (s % TT + 1) * P
                S0 = p * STEPS + s
                act.wait_ge(s_shifted, S0 + 1)
                ge(act, et_done, S0 - 1)
                nc.scalar.activation(E[:, s % 2, 0:n], S[:, s % 2, 0:n], ACT.Exp, bias=smin[:, s % 2:s % 2 + 1],
                                     scale=-1.0, accum_out=rsum[:, b, s:s + 1]).then_inc(e_done, 1)

            def copy_turned(p, s):
                n = (s % TT + 1) * P
                S0 = p * STEPS + s
                act.wait_ge(et_done, S0 + 1)
                ge(act, pv_done, S0 - 1)
                nc.scalar.activation(ET[:, s % 2, 0:n], ps_t[:, 0:n], ACT.Copy).then_inc(et_ready, 1)

            def out_upper(p):
                act.wait_ge(o_turned, p + 1)
                nc.scalar.activation(oh[:, bass.ds(p, 1), :].rearrange("p a t -> p (a t)"), ps_t[:, :], ACT.Copy)\
                    .then_inc(oh_done, 1)

            def queries_upper(p, b):
                act.wait_ge(tile_free, p * 2 + (TILE0["qk"] + 1))
                for a in range(2):
                    r = HALF[a]
                    ins = nc.scalar.activation(q_both[r, b, a, :], tmp[r, 0, :], ACT.Copy)
                ins.then_inc(qh_done, 1)

            def keys_upper(p, a, b):
                act.wait_ge(tile_free, p * 2 + (TILE0["qk"] + 2))
                for half in HALF:
                    ins = nc.scalar.activation(k_both[half, b, a, :], tmp[HALF[a], 1, :], ACT.Copy)
                ins.then_inc(kh_done, 1)

            def attend(p, b, first, last):
                split = upper_parts(b, p + (CHUNK0["qk"] + 2), KC, 3)
                for s in range(STEPS):
                    if s == 6 and not first:
                        out_upper(p - 1)
                    if s == STEPS - 1 and not last:
                        keys_upper(p + 1, 0, 1 - b)
                    exps(p, s, b)
                    if s >= 1:
                        copy_turned(p, s - 1)
                    elif not first:
                        copy_turned(p - 1, STEPS - 1)
                    next(split, None)
                    if s == 3 and not last:
                        queries_upper(p + 1, 1 - b)
                if not last:
                    keys_upper(p + 1, 1, 1 - b)
                else:
                    copy_turned(p, STEPS - 1)
                    out_upper(p)

            queries_upper(0, 0)
            for a in range(2):
                keys_upper(0, a, 0)
            attend(0, 0, True, False)
            with Loop(act, 0, PAIRS // 2 - 1) as i:
                attend(i * 2 + 1, 1, False, False)
                attend(i * 2 + 2, 0, False, False)
            attend(PAIRS - 1, 1, False, True)

            def residual_pass(name, norm, cuts):
                per = 2 * len(cuts)

                def half(i):
                    for n in range(per):
                        if n % len(cuts) == len(cuts) - 1:
                            if name == "ao" and n == 0:
                                upper(n % 2, i * per + (CHUNK0[name] + n + 2))
                            for e in range(2):
                                k = i * 4 + (n // len(cuts) * 2 + e)
                                residual(name, k, e, norm)
                        size = cuts[(n + 2) % len(cuts)] if n + 2 < per else KC
                        if name != "ao" or n > 0:
                            upper(n % 2, i * per + (CHUNK0[name] + n + 2), size)

                if RES0[name] == 0:
                    half(0)
                    half(1)
                else:
                    with Loop(act, 0, 2) as i:
                        half(i)

            def ffn_in(name, layer, norm):
                norm_root(norm)
                norm_rows(norm)
                with Loop(act, 0, KF // 2) as j:
                    for e in range(2):
                        act.wait_ge(tile_free, j * 4 + (TILE0[name] + e + 1))
                        nc.scalar.activation(tmp[:, e, :], tmp[:, e, :], ACT.Silu).then_inc(silu_done, 1)
                    upper(0, j * 2 + (CHUNK0[name] + 2))
                    for e in range(2):
                        act.wait_ge(tile_free, j * 4 + (TILE0[name] + e + 3))
                        nc.scalar.activation(ah[:, bass.ds(j * 2 + e, 1), :].rearrange("p a t -> p (a t)"),
                                             tmp[:, 2 + e, :], ACT.Copy).then_inc(ah_done, 1)
                    upper(1, j * 2 + (CHUNK0[name] + 3))

            residual_pass("ao", 1, (8,))
            ffn_in("in0", 0, 1)
            residual_pass("out0", 2, (8, 8, 6))

            norm_root(2)
            with Loop(act, 0, 4) as i:
                for b in range(2):
                    for t in range(TT):
                        act.wait_ge(tile_free, i * 4 + (TILE0["sv"] + 2 * b + t // 2 + 1))
                        v = vt[:, bass.ds(i * 4 + 2 * b, 2), t, :]
                        nc.scalar.activation(v, v, ACT.Gelu).then_inc(vg_done, 1)
                    upper(b, i * 2 + (CHUNK0["sv"] + b + 2))
            norm_rows(2)
            act.wait_ge(var_ready, 1)
            nc.scalar.activation(cols[:, 0, :], lncol[:, :, 1], ACT.Sqrt, bias=bias[:, 0:1]).then_inc(lnstd_done, 1)

            with Loop(act, 0, 4) as i:
                for b in range(2):
                    for e in range(2):
                        act.wait_ge(tile_free, i * 4 + (TILE0["su"] + 2 * b + e + 1))
                        nc.scalar.activation(tmp[:, e, :], tmp[:, e, :], ACT.Gelu).then_inc(u_done, 1)
                    upper(b, i * 2 + (CHUNK0["su"] + b + 2))
                    for e in range(2):
                        act.wait_ge(gated, i * 4 + (2 * b + e + 1))
                        nc.scalar.activation(gh[:, bass.ds(i * 4 + (2 * b + e), 1), :].rearrange("p a t -> p (a t)"),
                                             tmp[:, 2 + e, :], ACT.Copy).then_inc(gh_done, 1)
            residual_pass("so", 3, (8, 8))
            ffn_in("in1", 1, 3)

            for n in range(12):
                if n == 11:
                    nc.scalar.activation(cols[0:1, 2, 0:1], bias[0:1, 1:2], ACT.Sqrt)
                if n in (2, 5, 8):
                    for e in range(2):
                        k = n // 3 * 2 + e
                        residual("out1", k, e, 4)
                if n + 2 < 12:
                    upper(n % 2, CHUNK0["out1"] + n + 2, 6 if n % 3 == 0 else KC)
                if n == 0:
                    act.wait_ge(w_used, CHUNK0["out1"])
                    act.dma_start(fw[:, :], final_norm_w.rearrange("(a d) -> a d", a=1).partition_broadcast(P))\
                        .then_inc(fw_loaded, 16)

            def square_half(h, e):
                act.wait_ge(tile_free, TILE0["out1"] + 7 + 2 * h + e)
                act.wait_ge(sq_added, 4 * KD - 3 + e)
                c0, c1 = h * T // 2, (h + 1) * T // 2
                nc.scalar.activation(sq[:, e, c0:c1], xT[:, 6 + e, c0:c1], ACT.Square).then_inc(sq_done, 1)

            def root_half(h):
                act.wait_ge(mean_done, 5 + h)
                nc.scalar.activation(cols[:, 0, 2 * h:2 * h + 2], cols[:, 1, 2 * h:2 * h + 2], ACT.Sqrt)\
                    .then_inc(std_done, 1)

            def scale_tokens(t):
                act.wait_ge(r_done, 5 + t // 2)
                act.wait_ge(y_copied, 8 + t // 2 * 2)
                nc.scalar.activation(y[:, t, :], y[:, t, :], ACT.Copy, scale=rcol[:, t:t + 1]).then_inc(y_scaled_act, 1)

            square_half(0, 0)
            square_half(0, 1)
            square_half(1, 0)
            root_half(0)
            scale_tokens(1)
            square_half(1, 1)
            root_half(1)
            scale_tokens(3)

        @block.vector
        def _(dve):
            step = Count(dve_step)

            def chained(ins):
                dve.wait_ge(dve_step, step.inc(ins))

            def tile_of(buf, k):
                return buf[:, bass.ds(k, 1), :].rearrange("p a t -> p (a t)")

            def lower_parts(slot, n, ks=KC, parts=1):
                dve.wait_ge(w_hi, n + 1)
                ge(dve, w_used, n - 1)
                for q in range(parts):
                    k0, k1 = ks * q // parts, ks * (q + 1) // parts
                    ins = nc.vector.tensor_tensor(wl[:, slot, k0:k1, :], raw[:, slot, k0:k1, :],
                                                  wh[:, slot, k0:k1, :].bitcast(F32), ALU.subtract)
                    if q == parts - 1:
                        ins.then_inc(w_lo, 1)
                    yield

            def lower(slot, n, ks=KC):
                for _ in lower_parts(slot, n, ks):
                    pass

            def input_lower(r, k, norm):
                dve.wait_ge(xh_done, r + (KD + 1))
                nc.vector.scalar_tensor_tensor(out=tile_of(xl, k), in0=tile_of(xT, k),
                                               scalar=nw[:, bass.ds(k + NORM_ROW[norm], 1)],
                                               in1=tile_of(xh, k).bitcast(F32), op0=ALU.mult,
                                               op1=ALU.subtract).then_inc(xl_done, 1)

            def newton(out_, mean, root, r, t):
                chained(nc.vector.reciprocal(r, root))
                chained(nc.vector.tensor_tensor(t, r, r, ALU.mult))
                chained(nc.vector.tensor_tensor(t, t, mean, ALU.mult))
                chained(nc.vector.tensor_scalar(t, t, -0.5, 1.5, ALU.mult, ALU.add))
                return nc.vector.tensor_tensor(out_, r, t, ALU.mult)

            def norm_scale(norm):
                if norm > 0:
                    dve.wait_ge(summed, norm)
                else:
                    dve.wait_ge(xsq_done, TT)
                nc.vector.tensor_scalar(cols[:, 1, :], ps_s[1][:, 0:TT] if norm > 0 else xsq[:, :], 1.0 / D,
                                        NORM_EPS, ALU.mult, ALU.add).then_inc(mean_done, 1)
                dve.wait_ge(std_done, norm + 1)
                newton(rcol[:, :], cols[:, 1, :], cols[:, 0, :], cols[:, 2, :], cols[:, 3, :]).then_inc(r_done, 1)
                dve.wait_ge(r_done, norm + 1)

            dve.wait_ge(consts, 5)
            dve.wait_ge(nw_turned, 1)
            nc.vector.tensor_copy(nw[:, :], bank[0][:, 0:32]).then_inc(nw_ready, 1)
            dve.wait_ge(nw_ready, 1)
            for t in range(TT):
                for h in range(2):
                    dve.wait_ge(x_turned, 2 * t + h + 1)
                    ge(dve, xl_done, 2 * t + h - 3)
                    nc.vector.tensor_tensor(weighed(t, h), turned(t, h),
                                            nw[:, 4 * h:4 * h + 4].unsqueeze(2).broadcast_to([P, KD // 2, P]),
                                            ALU.mult).then_inc(x_weighed, 1)
                for h in range(2):
                    dve.wait_ge(xh_done, 2 * t + h + 1)
                    nc.vector.tensor_tensor(x_half(xl, t, h), weighed(t, h), x_half(xh, t, h).bitcast(F32),
                                            ALU.subtract).then_inc(xl_done, 1)
                if t == 0:
                    lower(0, 0)
            lower(1, 1)
            norm_scale(0)
            dve.wait_ge(wf_hi, 1)
            nc.vector.tensor_tensor(wfs[:, :, LOW:LOW + H], wf[:, :, 0:H], wfs[:, :, 0:H].bitcast(F32), ALU.subtract)\
                .then_inc(wf_lo, 1)

            def values(c, m):
                for t in range(TT):
                    if t % 2 == 0:
                        wait_tile(dve, t // 2, first_done, m // 2, w_used, c)
                    ins = nc.vector.tensor_scalar(V[:, t, c * CW:(c + 1) * CW],
                                                  dense[(m + t // 2) % 4][:, t % 2 * CW:(t % 2 + 1) * CW],
                                                  rcol[:, t:t + 1], None, ALU.mult)
                    if t % 2 == 1:
                        ins.then_inc(tile_free, 1)

            ones_row = ones[0:H, 0:1].broadcast_to([H, T])
            for c in range(4):
                values(c, TILE0["v"] + 2 * c)
                lower(c % 2, c + 2)
                if c == 1:
                    dve.wait_ge(f_done, 1)
                    dve.wait_ge(rms_done, 1)
                    nc.vector.tensor_tensor(fz[:, :], ps_o[0:H, :], rms[0:H, :], ALU.mult)
                    chained(nc.vector.tensor_tensor(fa[:, :], ps_o[LOW:LOW + H, :], rms[LOW:LOW + H, :], ALU.mult))
                    chained(nc.vector.tensor_tensor(fz[:, :], fz[:, :], fa[:, :], ALU.add))
                    chained(nc.vector.tensor_scalar(fz[:, :], fz[:, :], bf[:, 0:1], None, ALU.add))
                    nc.vector.scalar_tensor_tensor(out=fa[:, :], in0=fz[:, :], scalar=-1.0, in1=fz[:, :],
                                                   op0=ALU.mult, op1=ALU.max).then_inc(fz_done, 1)
                if c == 2:
                    dve.wait_ge(fe_done, 2)
                    chained(nc.vector.scalar_tensor_tensor(out=fz[:, :], in0=fz[:, :], scalar=0.0, in1=fa[:, :],
                                                           op0=ALU.min, op1=ALU.subtract))
                    nc.vector.tensor_tensor_scan(cT[:, :], ones_row, fz[:, :], 0.0, ALU.mult, ALU.add)\
                        .then_inc(c_ready, 1)

            def queries(p, b):
                dve.wait_ge(first_done, p + (TILE0["qk"] // 2 + 1))
                nc.vector.scalar_tensor_tensor(out=tmp[:, 0, :], in0=dense[2 * b][:, :], scalar=-(HD ** -0.5),
                                               in1=rms[:, :], op0=ALU.mult, op1=ALU.mult)\
                    .then_inc(tile_free, 1)

            def keys(p, b):
                dve.wait_ge(w_used, p + (CHUNK0["qk"] + 1))
                nc.vector.tensor_tensor(tmp[:, 1, :], dense[2 * b + 1][:, :], rms[:, :], ALU.mult)\
                    .then_inc(tile_free, 1)

            def queries_lower(p, b):
                dve.wait_ge(qh_done, p + 1)
                for a in range(2):
                    r, other = HALF[a], HALF[1 - a]
                    nc.vector.tensor_tensor(q_both[other, b, a, :], tmp[r, 0, :], q_both[r, b, a, :].bitcast(F32),
                                            ALU.subtract)

            def keys_lower(p, a, b):
                dve.wait_ge(kh_done, p * 2 + (a + 1))
                r = HALF[a]
                nc.vector.tensor_tensor(k_low[r, b, :], tmp[r, 1, :], k_both[r, b, a, :].bitcast(F32),
                                        ALU.subtract).then_inc(kl_done, 1)

            def shift(p, s, b):
                i, n = s % TT, (s % TT + 1) * P
                S0 = p * STEPS + s
                dve.wait_ge(s_done, S0 + 1)
                if s == 0:
                    dve.wait_ge(c_loaded[b], p * 8 + (16 - 8 * b))
                ge(dve, e_done, S0 - 1)
                apart(dve)
                nc.vector.tensor_tensor_reduce(S[:, s % 2, 0:n], ps_s[s % 2][:, 0:n], c_bc[:, b, s // TT, 0:n],
                                               1.0, 3.4e38, ALU.add, ALU.min, smin[:, s % 2:s % 2 + 1])\
                    .then_inc(s_shifted, 1)

            def normalised(p, a, b):
                dve.wait_ge(e_done, p * STEPS + (a + 1) * TT)
                chained(nc.vector.reciprocal(rinv[:, b, :], rsum[:, b, a * TT:(a + 1) * TT]))
                dve.wait_ge(pv_done, p * STEPS + (a + 1) * TT)
                if a == 0:
                    ge(dve, o_turned, p)
                nc.vector.tensor_tensor(o_tok[:, :, a * HD:(a + 1) * HD],
                                        ps_o[:, a * TT * HD:(a + 1) * TT * HD].rearrange("p (i d) -> p i d", d=HD),
                                        rinv[:, b, :].unsqueeze(2).broadcast_to([P, TT, HD]), ALU.mult)\
                    .then_inc(o_ready, 1)

            def out_lower(p):
                dve.wait_ge(oh_done, p + 1)
                nc.vector.tensor_tensor(tile_of(ol, p), ps_t[:, :], tile_of(oh, p).bitcast(F32), ALU.subtract)\
                    .then_inc(ol_done, 1)

            def attend(p, b, first, last):
                split = lower_parts(b, p + (CHUNK0["qk"] + 2), KC, 3)
                for s in range(STEPS):
                    if s == 6:
                        normalised(p, 0, b)
                        if not first:
                            out_lower(p - 1)
                    shift(p, s, b)
                    if s == 2 and not first:
                        normalised(p - 1, 1, 1 - b)
                    if s == 3 and not last:
                        queries(p + 1, 1 - b)
                    if s in (3, 4, 5):
                        next(split)
                    if s == 4 and not last:
                        queries_lower(p + 1, 1 - b)
                    if s == 6 and not last:
                        keys(p + 1, 1 - b)
                if not last:
                    for a in range(2):
                        keys_lower(p + 1, a, 1 - b)
                else:
                    normalised(p, 1, b)
                    out_lower(p)

            queries(0, 0)
            keys(0, 0)
            queries_lower(0, 0)
            for a in range(2):
                keys_lower(0, a, 0)
            attend(0, 0, True, False)
            with Loop(dve, 0, PAIRS // 2 - 1, own=[(step, 4)]) as i:
                attend(i * 2 + 1, 1, False, False)
                attend(i * 2 + 2, 0, False, False)
            attend(PAIRS - 1, 1, False, True)

            def gained(name, k, e, bank_, pair, chunk):
                wait_tile(dve, e, first_done, pair + TILE0[name] // 2, w_used, chunk + CHUNK0[name])
                nc.vector.tensor_tensor(tile_of(xT, k), tile_of(xT, k), dense[bank_][:, :], ALU.add)\
                    .then_inc(tile_free, 1)

            def residual_pass(name, norm, cuts):
                per = 2 * len(cuts)
                with Loop(dve, 0, 2) as i:
                    for n in range(per):
                        if n % len(cuts) == len(cuts) - 1:
                            for e in range(2):
                                t = n // len(cuts) * 2 + e
                                gained(name, i * 4 + t, e, t, i * 2 + t // 2, i * per + n)
                                if name != "ao" or n > 0:
                                    input_lower(i * 4 + (t + RES0[name]), i * 4 + t, norm)
                        size = cuts[(n + 2) % len(cuts)] if n + 2 < per else KC
                        lower(n % 2, i * per + (CHUNK0[name] + n + 2), size)
                        if name == "ao" and n == 0:
                            for k in range(2):
                                input_lower(i * 4 + (k + RES0[name]), i * 4 + k, norm)

            def ffn_in(name, layer, norm):
                norm_scale(norm)
                dve.wait_ge(rms_done, norm + 1)
                with Loop(dve, 0, KF // 2) as j:
                    for e in range(2):
                        wait_tile(dve, e, first_done, j * 2 + TILE0[name] // 2, w_used, j * 2 + CHUNK0[name])
                        nc.vector.tensor_tensor(tmp[:, e, :], dense[e][:, :], rms[:, :], ALU.mult)\
                            .then_inc(tile_free, 1)
                    lower(0, j * 2 + (CHUNK0[name] + 2))
                    for e in range(2):
                        wait_tile(dve, e, first_done, j * 2 + (TILE0[name] // 2 + 1), w_used,
                                  j * 2 + (CHUNK0[name] + 1))
                        dve.wait_ge(gr_done, j * 2 + (layer * KF + e + 1))
                        nc.vector.tensor_tensor(tmp[:, 2 + e, :], dense[2 + e][:, :], tmp[:, e, :], ALU.mult)\
                            .then_inc(tile_free, 1)
                    for e in range(2):
                        dve.wait_ge(ah_done, j * 2 + (layer * KF + e + 1))
                        nc.vector.tensor_tensor(tile_of(al, j * 2 + e), tmp[:, 2 + e, :],
                                                tile_of(ah, j * 2 + e).bitcast(F32), ALU.subtract)\
                            .then_inc(al_done, 1)
                    lower(1, j * 2 + (CHUNK0[name] + 3))

            residual_pass("ao", 1, (8,))
            ffn_in("in0", 0, 1)
            residual_pass("out0", 2, (8, 8, 6))

            norm_scale(2)

            def gate_v(i, turned):
                for b in range(2):
                    for t in range(TT):
                        if t % 2 == 0:
                            wait_tile(dve, t // 2, first_done, i * 2 + (TILE0["sv"] // 2 + b), w_used,
                                      i * 2 + (CHUNK0["sv"] + b))
                        ins = nc.vector.tensor_scalar(
                            vt[:, bass.ds(i * 4 + 2 * b, 2), t, :],
                            dense[2 * b + t // 2][:, t % 2 * CW:(t % 2 + 1) * CW].rearrange("p (g d) -> p g d", d=P),
                            rcol[:, t:t + 1], None, ALU.mult)
                        if t % 2 == 1:
                            ins.then_inc(tile_free, 1)
                    for t in range(TT):
                        dve.wait_ge(vg_done, i * (2 * TT) + (b * TT + t + 1))
                        ins = nc.vector.bn_stats(stats[:, t, bass.ds(i * 2 + b, 1), :].rearrange("p a s -> p (a s)"),
                                                 vt[:, bass.ds(i * 4 + 2 * b, 2), t, :])
                    ins.then_inc(stats_done, 1)
                    lower(b, i * 2 + (CHUNK0["sv"] + b + 2))
                    if turned:
                        for q in range(2 * b, 2 * b + 2):
                            dve.wait_ge(ws_turned, q + 1)
                            nc.vector.tensor_copy(wsT[:, 4 * q:4 * q + 4, :],
                                                  bank[6 + q % 2].rearrange("p (g t) -> p g t", t=P))\
                                .then_inc(ws_ready, 1)

            with Loop(dve, 0, 3) as i:
                gate_v(i, False)
            gate_v(3, True)
            dve.wait_ge(stats_done, 8)
            for t in range(TT):
                ins = nc.vector.bn_aggr(lncol[:, t, :], stats[:, t, :, :].rearrange("p c s -> p (c s)"))
            ins.then_inc(var_ready, 1)
            dve.wait_ge(var_ready, 1)
            chained(nc.vector.tensor_scalar(cols[:, 1, :], lncol[:, :, 1], LN_EPS, None, ALU.add))
            dve.wait_ge(lnstd_done, 1)
            chained(newton(rstd[:, :], cols[:, 1, :], cols[:, 0, :], cols[:, 2, :], cols[:, 3, :]))

            def centred(c):
                for t in range(TT):
                    v = vt[:, bass.ds(c * 2, 2), t, :]
                    nc.vector.tensor_scalar(v, v, lncol[:, t, 0:1], rstd[:, t:t + 1], ALU.subtract, ALU.mult)\
                        .then_inc(vc_done, 1)

            def gate(c, b, ahead):
                for e in range(2):
                    wait_tile(dve, e, first_done, c + TILE0["su"] // 2, w_used, c + CHUNK0["su"])
                    nc.vector.tensor_tensor(tmp[:, e, :], dense[2 * b + e][:, :], rms[:, :], ALU.mult)\
                        .then_inc(tile_free, 1)
                if ahead:
                    centred(c + 1)
                lower(b, c + (CHUNK0["su"] + 2))
                dve.wait_ge(ln_loaded[b], c * 24 + (48 - 24 * b))
                ge(dve, gl_done, c * 2)
                for e in range(2):
                    dve.wait_ge(mixed, c * 2 + (e + 1))
                    t = tmp[:, 2 + e, :].rearrange("p (c t) -> p c t", t=P)
                    nc.vector.tensor_tensor(t, ps_s[e].rearrange("p (c t) -> p c t", t=P),
                                            sbc[:, b, e * P:(e + 1) * P].unsqueeze(1).broadcast_to([P, TT, P]),
                                            ALU.add).then_inc(mix_read, 1)
                for e in range(2):
                    dve.wait_ge(mix_read, c * 2 + (e + 1))
                    dve.wait_ge(u_done, c * 2 + (e + 1))
                    nc.vector.tensor_tensor(tmp[:, 2 + e, :], tmp[:, 2 + e, :], tmp[:, e, :], ALU.mult)\
                        .then_inc(gated, 1)
                for e in range(2):
                    dve.wait_ge(gh_done, c * 2 + (e + 1))
                    nc.vector.tensor_tensor(tile_of(gl, c * 2 + e), tmp[:, 2 + e, :],
                                            tile_of(gh, c * 2 + e).bitcast(F32), ALU.subtract).then_inc(gl_done, 1)

            centred(0)
            gate(0, 0, True)
            gate(1, 1, True)
            with Loop(dve, 1, 3) as i:
                gate(i * 2, 0, True)
                gate(i * 2 + 1, 1, True)
            gate(6, 0, True)
            gate(7, 1, False)
            residual_pass("so", 3, (8, 8))
            ffn_in("in1", 1, 3)

            def result(k):
                dve.wait_ge(y_turned, k + 1)
                nc.vector.tensor_tensor(y[:, :, k * P:(k + 1) * P], bank[4 + k % 4].rearrange("p (t d) -> p t d", d=P),
                                        fw[:, k * P:(k + 1) * P].unsqueeze(1).broadcast_to([P, TT, P]), ALU.mult)\
                    .then_inc(y_copied, 1)

            for n in range(12):
                if n == 5:
                    dve.wait_ge(fw_loaded, 16)
                if n in (5, 8, 11):
                    for e in range(2):
                        result(n // 3 * 2 - 2 + e)
                if n in (2, 5, 8):
                    for e in range(2):
                        k = n // 3 * 2 + e
                        gained("out1", k, e, k % 4, k // 2, n)
                if n + 2 < 12:
                    lower(n % 2, CHUNK0["out1"] + n + 2, 6 if n % 3 == 0 else KC)

            def gained_half(h, e):
                dve.wait_ge(half_done, 2 * h + e + 1)
                c0, c1 = h * T // 2, (h + 1) * T // 2
                nc.vector.tensor_tensor(xT[:, 6 + e, c0:c1], xT[:, 6 + e, c0:c1], last_bank(h, e)[:, 0:T // 2],
                                        ALU.add).then_inc(tile_free, 1)

            def result_half(h, e):
                dve.wait_ge(y_turned, 7 + 2 * h + e)
                c0, c1 = (6 + e) * P, (7 + e) * P
                nc.vector.tensor_tensor(y[:, 2 * h:2 * h + 2, c0:c1],
                                        turned_half(h, e)[:, 0:T // 2].rearrange("p (t d) -> p t d", d=P),
                                        fw[:, c0:c1].unsqueeze(1).broadcast_to([P, TT // 2, P]), ALU.mult)\
                    .then_inc(y_copied, 1)

            def scale_half(h):
                r = slice(2 * h, 2 * h + 2)
                dve.wait_ge(summed, 4 + h)
                nc.vector.tensor_scalar(cols[:, 1, r], last_bank(0, h)[:, 0:TT // 2], 1.0 / D, NORM_EPS, ALU.mult,
                                        ALU.add).then_inc(mean_done, 1)
                dve.wait_ge(std_done, 5 + h)
                newton(rcol[:, r], cols[:, 1, r], cols[:, 0, r], cols[:, 2, r], cols[:, 3, r]).then_inc(r_done, 1)
                dve.wait_ge(r_done, 5 + h)
                dve.wait_ge(y_copied, 8 + 2 * h)
                nc.vector.tensor_scalar(y[:, 2 * h, :], y[:, 2 * h, :], rcol[:, 2 * h:2 * h + 1], None, ALU.mult)\
                    .then_inc(y_scaled_dve, 1)

            gained_half(0, 0)
            gained_half(0, 1)
            gained_half(1, 0)
            for e in range(2):
                result_half(0, e)
            scale_half(0)
            gained_half(1, 1)
            for e in range(2):
                result_half(1, e)
            scale_half(1)

        @block.tensor
        def _(pe):
            def product(out_, a, b, start, stop):
                nc.tensor.matmul(out_, a[0], b[1], start=start, stop=False)
                nc.tensor.matmul(out_, a[1], b[0], start=False, stop=False)
                return nc.tensor.matmul(out_, a[0], b[0], start=False, stop=stop)

            def w(slot, k, c0, c1):
                return wh[:, slot, k, c0:c1], wl[:, slot, k, c0:c1]

            def by_features(m, b, slot, e, ks, hi, lo, k0=0, first=True, last=True, ready=None):
                if first:
                    ge(pe, tile_free, m - 3)
                for k in range(ks):
                    if ready is not None:
                        pe.wait_ge(ready[0], ready[1] + k0 + k + 1)
                    ins = product(dense[b][:, :], w(slot, k, e * P, (e + 1) * P), (hi[:, k0 + k, :], lo[:, k0 + k, :]),
                                  first and k == 0, last and k == ks - 1)
                if last and e == 0:
                    ins.then_inc(first_done, 1)
                return ins

            def by_tokens(m, b, slot, ready=None, inputs=False):
                for t in range(TT):
                    if inputs and t == 1:
                        turn_input(TT - 1)
                    if t % 2 == 0:
                        ge(pe, tile_free, m + (t // 2 - 3))
                    for k in range(KD):
                        if ready is not None and t == 0:
                            pe.wait_ge(ready[0], ready[1] + k + 1)
                        if inputs and k % 4 == 0:
                            pe.wait_ge(xl_done, 2 * t + k // 4 + 1)
                        ins = product(dense[b + t // 2][:, t % 2 * CW:(t % 2 + 1) * CW],
                                      (xh[:, k, t * P:(t + 1) * P], xl[:, k, t * P:(t + 1) * P]), w(slot, k, 0, CW),
                                      k == 0, k == KD - 1)
                    if t == 1:
                        ins.then_inc(first_done, 1)
                return ins

            def chunk_ready(n):
                pe.wait_ge(w_lo, n + 1)

            def norm_sums(norm):
                pe.wait_ge(sq_added, KD * norm)
                for t in range(TT):
                    ins = nc.tensor.matmul(ps_s[1][:, t:t + 1], sqsum[:, t * P:(t + 1) * P], ones[:, 0:1],
                                           start=True, stop=True)
                ins.then_inc(summed, 1)

            def norm_spread(norm):
                pe.wait_ge(r_done, norm + 1)
                for t in range(TT):
                    ins = nc.tensor.matmul(ps_s[0][:, t * P:(t + 1) * P], rcol[:, t:t + 1].broadcast_to([P, P]),
                                           ident[:, :], start=True, stop=True)
                ins.then_inc(spread, 1)

            pe.wait_ge(consts, 5)
            pe.wait_ge(nw_loaded, 32)
            nc.tensor.transpose(bank[0][:, 0:32], nw_rows[:, :], ident[0:32, 0:32]).then_inc(nw_turned, 1)
            pe.wait_ge(nw_ready, 1)

            def turn_input(t):
                pe.wait_ge(x_loaded[t], 16)
                for h in range(2):
                    ge(pe, x_done, 2 * t + h - 3)
                    for k in range(KD // 2):
                        ins = nc.tensor.transpose(turned(t, h)[:, k, :],
                                                  x_tok[:, t, (4 * h + k) * P:(4 * h + k + 1) * P], ident[:, :])
                    ins.then_inc(x_turned, 1)

            for t in range(TT - 1):
                turn_input(t)

            for c in range(4):
                chunk_ready(c)
                by_tokens(TILE0["v"] + 2 * c, 2 * (c % 2), c % 2, inputs=c == 0).then_inc(w_used, 1)
                if c == 1:
                    pe.wait_ge(x_done, 2 * TT)
                    norm_spread(0)
                    pe.wait_ge(wf_lo, 1)
                    for k in range(KD):
                        nc.tensor.matmul(ps_o[:, :], wfs[:, k, :], xl[:, k, :], start=k == 0, stop=False)
                        ins = nc.tensor.matmul(ps_o[:, :], wfs[:, k, :], xh[:, k, :], start=False, stop=k == KD - 1)
                    ins.then_inc(f_done, 1)

            def qk_part(p, b, part):
                e, q = part // TT, part % TT
                m = p * 2 + (TILE0["qk"] + e)
                if part == 0:
                    chunk_ready(p + CHUNK0["qk"])
                if q == 0:
                    ge(pe, tile_free, m - 3)
                for k in range(2 * q, 2 * q + 2):
                    ins = product(dense[2 * b + e][:, :], w(b, k, e * P, (e + 1) * P), (xh[:, k, :], xl[:, k, :]),
                                  k == 0, k == KD - 1)
                if q == TT - 1:
                    ins.then_inc((first_done, w_used)[e], 1)

            def scores(p, s, b):
                a, i, n = s // TT, s % TT, (s % TT + 1) * P
                S0 = p * STEPS + s
                if i == 0:
                    pe.wait_ge(kl_done, p * 2 + (a + 1))
                ge(pe, s_shifted, S0 - 1)
                r = slice(a * HD, (a + 1) * HD)
                nc.tensor.matmul(ps_s[s % 2][:, 0:n], q_both[:, b, a, i * P:(i + 1) * P], k_both[:, b, a, 0:n],
                                 start=True, stop=False, skip_group_check=True)
                nc.tensor.matmul(ps_s[s % 2][:, 0:n], q_both[r, b, a, i * P:(i + 1) * P], k_low[r, b, 0:n],
                                 start=False, stop=False, skip_group_check=True)
                nc.tensor.matmul(ps_s[s % 2][:, i * P:n], identr[:, :], mask[:, :],
                                 start=False, stop=True, skip_group_check=True).then_inc(s_done, 1)

            def turn(p, s, after_out=False):
                S0 = p * STEPS + s
                pe.wait_ge(e_done, S0 + 1)
                if after_out:
                    pe.wait_ge(ol_done, p)
                ge(pe, et_ready, S0)
                for j in range(s % TT + 1):
                    ins = nc.tensor.transpose(ps_t[:, j * P:(j + 1) * P], E[:, s % 2, j * P:(j + 1) * P], ident[:, :])
                ins.then_inc(et_done, 1)

            def weigh(p, s):
                a, i = s // TT, s % TT
                S0 = p * STEPS + s
                pe.wait_ge(et_ready, S0 + 1)
                ge(pe, o_ready, p * 2 + a)
                for j in range(i + 1):
                    ins = nc.tensor.matmul(ps_o[:, s * HD:(s + 1) * HD], ET[:, s % 2, j * P:(j + 1) * P],
                                           V[:, j, bass.ds(p * P + a * HD, HD)], start=(j == 0), stop=(j == i))
                ins.then_inc(pv_done, 1)

            def turn_out(p, S1):
                pe.wait_ge(o_ready, p * 2 + 2)
                pe.wait_ge(et_ready, S1)
                for t in range(TT):
                    ins = nc.tensor.transpose(ps_t[:, t * P:(t + 1) * P], o_tok[:, t, :], ident[:, :])
                ins.then_inc(o_turned, 1)

            def attend(p, b, first, last):
                for s in range(STEPS):
                    if s >= 3:
                        weigh(p, s - 3)
                    elif s > 0 and not first:
                        weigh(p - 1, s + STEPS - 3)
                    if s == 0 and not last:
                        qk_part(p + 1, 1 - b, 0)
                        if first:
                            qk_part(p + 1, 1 - b, 1)
                    elif s == 0:
                        out_part(0, 0, 2)
                    if s == 6 and not first:
                        turn_out(p - 1, p * STEPS + 5)
                    scores(p, s, b)
                    if not last and s < STEPS - 1 and not (first and s == 0):
                        qk_part(p + 1, 1 - b, s + 1)
                    elif last and s == 6:
                        out_part(1, 0, 2)
                    elif last and s > 0:
                        out_part(0, 2 * min(s, 6), 2 * min(s, 6) + 2)
                    if s == STEPS - 1:
                        weigh(p, s - 2)
                    if s >= 1:
                        turn(p, s - 1, s == 6 and not first)
                    elif not first:
                        turn(p - 1, STEPS - 1)

            def out_part(c, first, end):
                n = CHUNK0["ao"] + c
                for u in range(first, end):
                    k, e = u // 2, u % 2
                    if u == 0:
                        chunk_ready(n)
                    if k == 0:
                        ge(pe, tile_free, TILE0["ao"] + 2 * c + e - 3)
                    pe.wait_ge(ol_done, k + 1)
                    ins = product(dense[2 * c + e][:, :], w(c, k, e * P, (e + 1) * P), (oh[:, k, :], ol[:, k, :]),
                                  k == 0, k == KD - 1)
                    if k == KD - 1:
                        ins.then_inc((first_done, w_used)[e], 1)

            pe.wait_ge(mask_ready, 2)
            for part in range(STEPS):
                qk_part(0, 0, part)
            attend(0, 0, True, False)
            with Loop(pe, 0, PAIRS // 2 - 1) as i:
                attend(i * 2 + 1, 1, False, False)
                attend(i * 2 + 2, 0, False, False)
            attend(PAIRS - 1, 1, False, True)
            out_part(1, 2, 4)
            turn(PAIRS - 1, STEPS - 1)
            weigh(PAIRS - 1, STEPS - 2)
            out_part(1, 4, 5)
            weigh(PAIRS - 1, STEPS - 1)
            out_part(1, 5, 7)
            turn_out(PAIRS - 1, PAIRS * STEPS)
            out_part(1, 7, 9)
            out_part(0, 14, 16)
            out_part(1, 9, 16)

            def residual_pass(name, cuts, hi, lo, ready, i, after_first=None):
                per = 2 * len(cuts)
                n = 0
                for b in range(2):
                    k0 = 0
                    for q, ks in enumerate(cuts):
                        chunk_ready(i * per + (CHUNK0[name] + n))
                        for e in range(2):
                            ins = by_features(i * 4 + (TILE0[name] + 2 * b + e), 2 * b + e, n % 2, e, ks, hi, lo, k0,
                                              q == 0, q == len(cuts) - 1, ready)
                        ins.then_inc(w_used, 1)
                        if n == 0 and after_first:
                            after_first()
                        k0 += ks
                        n += 1

            def ffn_in_chunk(name, j, half, ready=None, between=None):
                chunk_ready(j * 2 + (CHUNK0[name] + half))
                for e in range(2):
                    if e == 1 and between:
                        between()
                    ins = by_features(j * 4 + (TILE0[name] + 2 * half + e), 2 * half + e, half, e, KC, xh, xl,
                                      ready=ready if e == 0 else None)
                ins.then_inc(w_used, 1)

            def ffn_in(name, norm):
                ffn_in_chunk(name, 0, 0, (xl_done, KD * norm), lambda: norm_sums(norm))
                norm_spread(norm)
                ffn_in_chunk(name, 0, 1)
                with Loop(pe, 1, KF // 2) as j:
                    ffn_in_chunk(name, j, 0)
                    ffn_in_chunk(name, j, 1)

            residual_pass("ao", (8,), oh, ol, None, 1)
            ffn_in("in0", 1)
            with Loop(pe, 0, 2) as i:
                residual_pass("out0", (8, 8, 6), ah, al, (al_done, 0), i)

            def gate_v(c, b, ready=None):
                chunk_ready(c + CHUNK0["sv"])
                by_tokens(c * 2 + TILE0["sv"], 2 * b, b, ready).then_inc(w_used, 1)

            gate_v(0, 0, (xl_done, KD * 2))
            norm_sums(2)
            gate_v(1, 1)
            norm_spread(2)
            with Loop(pe, 1, 3) as i:
                gate_v(i * 2, 0)
                gate_v(i * 2 + 1, 1)
            pe.wait_ge(ws_masked, 1)
            for c in (6, 7):
                gate_v(c, c - 6)
                for q in range(2 * (c - 6), 2 * (c - 6) + 2):
                    ge(pe, ws_ready, q - 1)
                    for g in range(4):
                        ins = nc.tensor.transpose(bank[6 + q % 2][:, g * P:(g + 1) * P], ws[:, 4 * q + g, :],
                                                  ident[:, :])
                    ins.then_inc(ws_turned, 1)

            def gate_u(c, b):
                chunk_ready(c + CHUNK0["su"])
                for e in range(2):
                    ins = by_features(c * 2 + (TILE0["su"] + e), 2 * b + e, b, e, KC, xh, xl)
                ins.then_inc(w_used, 1)

            def mix(c):
                for e in range(2):
                    pe.wait_ge(vn_done, c * 2 + (e + 1))
                    ge(pe, mix_read, c * 2 + (e - 1))
                    for t in range(TT):
                        ins = nc.tensor.matmul(ps_s[e][:, t * P:(t + 1) * P], vt[:, c * 2 + e, t, :],
                                               wsT[:, c * 2 + e, :], start=True, stop=True)
                    ins.then_inc(mixed, 1)

            gate_u(0, 0)
            pe.wait_ge(ws_ready, 4)
            for c in range(1, 8):
                gate_u(c, c % 2)
                mix(c - 1)
            residual_pass("so", (8, 8), gh, gl, (gl_done, 0), 0, lambda: mix(7))
            residual_pass("so", (8, 8), gh, gl, (gl_done, 0), 1)
            ffn_in("in1", 3)
            def turn_back(k):
                pe.wait_ge(tile_free, TILE0["out1"] + k + 1)
                ge(pe, y_copied, k - 3)
                for t in range(TT):
                    ins = nc.tensor.transpose(bank[4 + k % 4][:, t * P:(t + 1) * P], xT[:, k, t * P:(t + 1) * P],
                                              ident[:, :])
                ins.then_inc(y_turned, 1)

            for g in range(3):
                k0 = 0
                for q, ks in enumerate((8, 8, 6)):
                    n = 3 * g + q
                    chunk_ready(CHUNK0["out1"] + n)
                    for e in range(2):
                        k = 2 * g + e
                        ins = by_features(TILE0["out1"] + k, k % 4, n % 2, e, ks, ah, al, k0, q == 0, q == 2,
                                          (al_done, KF))
                        if e == 1:
                            ins.then_inc(w_used, 1)
                        if q == 1 and g > 0:
                            turn_back(2 * g - 2 + e)
                    k0 += ks

            def last_part(n, h, e, ks, k0):
                if n == 0:
                    pe.wait_ge(tile_free, TILE0["out1"] + (3, 5)[h] + e)
                c0, c1 = h * T // 2, (h + 1) * T // 2
                for k in range(ks):
                    ins = product(last_bank(h, e)[:, 0:T // 2], w((9 + n) % 2, k, e * P, (e + 1) * P),
                                  (ah[:, k0 + k, c0:c1], al[:, k0 + k, c0:c1]), n == 0 and k == 0,
                                  n == 2 and k == ks - 1)
                return ins

            def finish(h):
                for e in range(2):
                    pe.wait_ge(tile_free, TILE0["out1"] + 7 + 2 * h + e)
                    for t in range(TT // 2):
                        c = (2 * h + t) * P
                        ins = nc.tensor.transpose(turned_half(h, e)[:, t * P:(t + 1) * P], xT[:, 6 + e, c:c + P],
                                                  ident[:, :])
                    ins.then_inc(y_turned, 1)
                pe.wait_ge(sq_added, 4 * KD - 2)
                pe.wait_ge(sq_done, 4 * KD + 2 * h)
                for t in range(TT // 2):
                    c = (2 * h + t) * P
                    for m, squares in enumerate((sqsum[:, c:c + P], sq[:, 0, c:c + P], sq[:, 1, c:c + P])):
                        ins = nc.tensor.matmul(last_bank(0, h)[:, t:t + 1], squares, ones[:, 0:1],
                                               start=m == 0, stop=m == 2)
                ins.then_inc(summed, 1)

            k0 = 0
            for n, ks in enumerate((8, 8, 6)):
                chunk_ready(CHUNK0["out1"] + 9 + n)
                for h in range(2):
                    for e in range(2):
                        ins = last_part(n, h, e, ks, k0)
                        if n == 1 and h == 1:
                            turn_back(4 + e)
                        if n == 2:
                            ins.then_inc(half_done, 1)
                        elif h == 1 and e == 1:
                            ins.then_inc(w_used, 1)
                        if n == 2 and h == 1 and e == 0:
                            pe.wait_ge(y_copied, 6)
                            finish(0)
                k0 += ks
            finish(1)


_INPUTS = ["x", "mixer_norm_w", "attn_w_in", "attn_b_f", "attn_w_out", "sgu_w_in", "sgu_ln_g", "sgu_ln_b",
           "sgu_w_s", "sgu_b_s", "sgu_w_out", "ffn_norm_w", "ffn_w_in", "ffn_w_out", "final_norm_w"]


def kernel(**inputs):
    import numpy as np
    import concourse.bacc as bacc
    from concourse.bass_utils import run_bass_kernel_spmd

    nc = bacc.Bacc("TRN2", target_bir_lowering=False, num_devices=1)
    arrays, args = {}, []
    for name in _INPUTS:
        a = np.ascontiguousarray(inputs[name])
        arrays[f"in_{name}"] = a
        args.append(nc.dram_tensor(f"in_{name}", a.shape, mybir.dt.from_np(a.dtype), kind="ExternalInput").ap())
    shape = arrays["in_x"].shape
    args.append(nc.dram_tensor("trunk_out", shape, F32, kind="ExternalOutput").ap())
    trunk_kernel(nc, *args)
    r = run_bass_kernel_spmd(nc, [arrays], core_ids=[0])
    return r.results[0]["trunk_out"]
```
